# Optimizing a Trainium2 kernel written in Bass

```python
import math
import jax, jax.numpy as jnp
from jax import lax
import numpy as np
import jax
import jax.numpy as jnp

D_MODEL = 1024
BATCH = 1
SEQ = 256
DEPTH = 2

MEM_LEN = 256
HEAD_DIM = 64
DIFF_HEADS = 4
DIFF_QK = 32
DIFF_V = 2 * DIFF_QK
MLA_HEADS = 4
MLA_Q_RANK = 256
MLA_KV_RANK = 128
MLA_NOPE = 64
MLA_ROPE = 32
MLA_V = 64
SWA_Q_HEADS = 8
SWA_KV_HEADS = 2
SWA_GROUP = SWA_Q_HEADS // SWA_KV_HEADS
SWA_WINDOW = 128
D_MIX = DIFF_HEADS * DIFF_V + MLA_HEADS * MLA_V + SWA_Q_HEADS * HEAD_DIM
IN_SIZES = [DIFF_HEADS * 2 * DIFF_QK, DIFF_HEADS * 2 * DIFF_QK, DIFF_HEADS * DIFF_V,
            MLA_Q_RANK, MLA_KV_RANK, MLA_ROPE,
            SWA_Q_HEADS * HEAD_DIM, SWA_KV_HEADS * HEAD_DIM, SWA_KV_HEADS * HEAD_DIM]
D_IN = sum(IN_SIZES)
IN_SPLITS = [int(v) for v in np.cumsum(IN_SIZES)[:-1]]
X_HEADS = 4
X_HEAD_DIM = D_MODEL // X_HEADS
D_FF = -(-8 * D_MODEL // (3 * 256)) * 256

N_ALIBI = DIFF_HEADS + SWA_Q_HEADS
QBLK = 128
ROPE_THETA = 10000.0
EPS = 1e-6


def rmsnorm(x, g):
    xf = x.astype(jnp.float32)
    y = xf * lax.rsqrt(jnp.mean(xf * xf, axis=-1, keepdims=True) + EPS)
    return (y * g.astype(jnp.float32)).astype(x.dtype)

def rope(x, pos):
    half = x.shape[-1] // 2
    inv = ROPE_THETA ** (-jnp.arange(half, dtype=jnp.float32) / half)
    ang = pos.astype(jnp.float32)[..., None] * inv
    ang = ang.reshape(ang.shape[:2] + (1,) * (x.ndim - 3) + (half,))
    cos, sin = jnp.cos(ang), jnp.sin(ang)
    xf = x.astype(jnp.float32)
    x1, x2 = xf[..., :half], xf[..., half:]
    return jnp.concatenate([x1 * cos - x2 * sin, x1 * sin + x2 * cos], axis=-1).astype(x.dtype)

def alibi_slopes():
    return 2.0 ** (-8.0 * jnp.arange(1, N_ALIBI + 1, dtype=jnp.float32) / N_ALIBI)

def diff_attention(q, k, v, pos, slopes, lam):
    B, S, H, _ = q.shape
    nblk = S // QBLK
    scale = 1.0 / math.sqrt(DIFF_QK)
    qb = q.reshape(B, nblk, QBLK, H, 2, DIFF_QK).swapaxes(0, 1)
    pb = pos.reshape(B, nblk, QBLK).swapaxes(0, 1)
    k2 = k.reshape(B, S, H, 2, DIFF_QK)

    def one_block(args):
        qi, pi = args
        s = jnp.einsum('bqhmd,bshmd->bmhqs', qi, k2).astype(jnp.float32) * scale
        dist = jnp.abs(pi[:, :, None] - pos[:, None, :]).astype(jnp.float32)
        s = s - slopes[None, None, :, None, None] * dist[:, None, None]
        p = jax.nn.softmax(s, axis=-1)
        a = p[:, 0] - lam * p[:, 1]
        return jnp.einsum('bhqs,bshd->bqhd', a.astype(v.dtype), v)

    out = lax.map(one_block, (qb, pb))
    return out.swapaxes(0, 1).reshape(B, S, H, DIFF_V)

def mla_attention(q, k, v):
    B, S, H, D = q.shape
    nblk = S // QBLK
    scale = 1.0 / math.sqrt(D)
    qb = q.reshape(B, nblk, QBLK, H, D).swapaxes(0, 1)

    def one_block(qi):
        s = jnp.einsum('bqhd,bshd->bhqs', qi, k).astype(jnp.float32) * scale
        p = jax.nn.softmax(s, axis=-1)
        return jnp.einsum('bhqs,bshd->bqhd', p.astype(v.dtype), v)

    out = lax.map(one_block, qb)
    return out.swapaxes(0, 1).reshape(B, S, H * MLA_V)

def swa_attention(q, k, v, pos, slopes, sinks):
    B, S = q.shape[:2]
    W = SWA_WINDOW
    nblk = S // W
    scale = 1.0 / math.sqrt(HEAD_DIM)

    def band(t):
        pad = [(0, 0), (W, W)] + [(0, 0)] * (t.ndim - 2)
        tp = jnp.pad(t, pad).reshape((t.shape[0], nblk + 2, W) + t.shape[2:])
        return jnp.concatenate([tp[:, :-2], tp[:, 1:-1], tp[:, 2:]], axis=2)

    kb, vb, pkb = band(k), band(v), band(pos)
    valid = band(jnp.ones((1, S), dtype=bool))
    qg = q.reshape(B, nblk, W, SWA_KV_HEADS, SWA_GROUP, HEAD_DIM)
    s = jnp.einsum('bnqkgd,bnskd->bnkgqs', qg, kb).astype(jnp.float32) * scale
    pq = pos.reshape(B, nblk, W)
    dist = jnp.abs(pq[..., :, None] - pkb[..., None, :]).astype(jnp.float32)
    s = s - slopes.reshape(SWA_KV_HEADS, SWA_GROUP)[:, :, None, None] * dist[:, :, None, None]
    offs = jnp.arange(3 * W)[None, :] - W - jnp.arange(W)[:, None]
    mask = (jnp.abs(offs) <= W)[None, None] & valid[:, :, None, :]
    s = jnp.where(mask[:, :, None, None], s, jnp.finfo(jnp.float32).min)
    sink = sinks.astype(jnp.float32).reshape(SWA_KV_HEADS, SWA_GROUP)[:, :, None, None]
    m = jnp.maximum(jnp.max(s, axis=-1, keepdims=True), sink)
    e = jnp.exp(s - m)
    p = e / (jnp.sum(e, axis=-1, keepdims=True) + jnp.exp(sink - m))
    o = jnp.einsum('bnkgqs,bnskd->bnqkgd', p.astype(v.dtype), vb)
    return o.reshape(B, S, SWA_Q_HEADS * HEAD_DIM)

def cross_attention(h, mem_n, w_q, w_kv, w_o):
    B, S, _ = h.shape
    M = mem_n.shape[1]
    q = (h @ w_q).reshape(B, S, X_HEADS, X_HEAD_DIM)
    k, v = jnp.split(mem_n @ w_kv, 2, axis=-1)
    k = k.reshape(B, M, X_HEADS, X_HEAD_DIM)
    v = v.reshape(B, M, X_HEADS, X_HEAD_DIM)
    s = jnp.einsum('bqhd,bmhd->bhqm', q, k).astype(jnp.float32) / math.sqrt(X_HEAD_DIM)
    p = jax.nn.softmax(s, axis=-1)
    o = jnp.einsum('bhqm,bmhd->bqhd', p.astype(v.dtype), v).reshape(B, S, D_MODEL)
    return o @ w_o

def first_inputs(seed: int = 0) -> dict:
    key = jax.random.key(seed)
    ks = jax.random.split(key, 32)
    f32 = jnp.float32

    def w(k, shape, fan_in):
        return jax.random.normal(k, shape, f32) * fan_in ** -0.5

    def gain(k, shape):
        return 1.0 + 0.02 * jax.random.normal(k, shape, f32)

    offset = jax.random.randint(ks[2], (BATCH, 1), 0, 1024, dtype=jnp.int32)
    positions = offset + jnp.arange(SEQ, dtype=jnp.int32)[None, :]
    return {
        "x": jax.random.normal(ks[0], (BATCH, SEQ, D_MODEL), f32),
        "mem": jax.random.normal(ks[1], (BATCH, MEM_LEN, D_MODEL), f32),
        "positions": positions,
        "g_mix_pre": gain(ks[3], (DEPTH, D_MODEL)),
        "g_mix_post": gain(ks[4], (DEPTH, D_MODEL)),
        "w_in": w(ks[5], (DEPTH, D_MODEL, D_IN), D_MODEL),
        "diff_lambda": 0.1 * jax.random.normal(ks[6], (DEPTH, 4, DIFF_QK), f32),
        "diff_head_g": gain(ks[7], (DEPTH, DIFF_V)),
        "mla_q_norm_g": gain(ks[8], (DEPTH, MLA_Q_RANK)),
        "mla_w_q_up": w(ks[9], (DEPTH, MLA_Q_RANK, MLA_HEADS * (MLA_NOPE + MLA_ROPE)), MLA_Q_RANK),
        "mla_kv_norm_g": gain(ks[10], (DEPTH, MLA_KV_RANK)),
        "mla_w_kv_up": w(ks[11], (DEPTH, MLA_KV_RANK, MLA_HEADS * (MLA_NOPE + MLA_V)), MLA_KV_RANK),
        "swa_sinks": 0.5 * jax.random.normal(ks[12], (DEPTH, SWA_Q_HEADS), f32),
        "w_out": w(ks[13], (DEPTH, D_MIX, D_MODEL), D_MIX),
        "g_x_pre": gain(ks[14], (DEPTH, D_MODEL)),
        "g_x_mem": gain(ks[15], (DEPTH, D_MODEL)),
        "g_x_post": gain(ks[16], (DEPTH, D_MODEL)),
        "w_xq": w(ks[17], (DEPTH, D_MODEL, D_MODEL), D_MODEL),
        "w_xkv": w(ks[18], (DEPTH, D_MODEL, 2 * D_MODEL), D_MODEL),
        "w_xo": w(ks[19], (DEPTH, D_MODEL, D_MODEL), D_MODEL),
        "g_ffn_pre": gain(ks[20], (DEPTH, D_MODEL)),
        "g_ffn_post": gain(ks[21], (DEPTH, D_MODEL)),
        "w_ffn_in": w(ks[22], (DEPTH, D_MODEL, 2 * D_FF), D_MODEL),
        "w_ffn_out": w(ks[23], (DEPTH, D_FF, D_MODEL), D_FF),
    }

def first_block(x, mem, positions, g_mix_pre, g_mix_post, w_in, diff_lambda, diff_head_g,
              mla_q_norm_g, mla_w_q_up, mla_kv_norm_g, mla_w_kv_up, swa_sinks, w_out,
              g_x_pre, g_x_mem, g_x_post, w_xq, w_xkv, w_xo,
              g_ffn_pre, g_ffn_post, w_ffn_in, w_ffn_out):
    B, S, _ = x.shape
    slopes = alibi_slopes()
    swa_slopes = slopes[:SWA_Q_HEADS]
    diff_slopes = slopes[SWA_Q_HEADS:]

    for l in range(DEPTH):
        h = rmsnorm(x, g_mix_pre[l])
        (a_q, a_k, a_v, b_cq, b_ckv, b_kr, c_q, c_k, c_v) = jnp.split(h @ w_in[l], IN_SPLITS, axis=-1)

        lam_init = 0.8 - 0.6 * math.exp(-0.3 * l)
        lp = diff_lambda[l].astype(jnp.float32)
        lam = jnp.exp(jnp.sum(lp[0] * lp[1])) - jnp.exp(jnp.sum(lp[2] * lp[3])) + lam_init
        o_a = diff_attention(a_q.reshape(B, S, DIFF_HEADS, 2 * DIFF_QK),
                             a_k.reshape(B, S, DIFF_HEADS, 2 * DIFF_QK),
                             a_v.reshape(B, S, DIFF_HEADS, DIFF_V),
                             positions, diff_slopes, lam)
        o_a = (rmsnorm(o_a, diff_head_g[l]) * (1.0 - lam_init)).reshape(B, S, DIFF_HEADS * DIFF_V)

        qb = (rmsnorm(b_cq, mla_q_norm_g[l]) @ mla_w_q_up[l]).reshape(B, S, MLA_HEADS, MLA_NOPE + MLA_ROPE)
        qb = jnp.concatenate([qb[..., :MLA_NOPE], rope(qb[..., MLA_NOPE:], positions)], axis=-1)
        kvb = (rmsnorm(b_ckv, mla_kv_norm_g[l]) @ mla_w_kv_up[l]).reshape(B, S, MLA_HEADS, MLA_NOPE + MLA_V)
        k_rope = jnp.broadcast_to(rope(b_kr, positions)[:, :, None, :], (B, S, MLA_HEADS, MLA_ROPE))
        kb = jnp.concatenate([kvb[..., :MLA_NOPE], k_rope], axis=-1)
        o_b = mla_attention(qb, kb, kvb[..., MLA_NOPE:])

        o_c = swa_attention(c_q.reshape(B, S, SWA_Q_HEADS, HEAD_DIM),
                            c_k.reshape(B, S, SWA_KV_HEADS, HEAD_DIM),
                            c_v.reshape(B, S, SWA_KV_HEADS, HEAD_DIM),
                            positions, swa_slopes, swa_sinks[l])

        mix = jnp.concatenate([o_a, o_b, o_c], axis=-1) @ w_out[l]
        x = x + rmsnorm(mix, g_mix_post[l])

        xo = cross_attention(rmsnorm(x, g_x_pre[l]), rmsnorm(mem, g_x_mem[l]), w_xq[l], w_xkv[l], w_xo[l])
        x = x + rmsnorm(xo, g_x_post[l])

        gate, up = jnp.split(rmsnorm(x, g_ffn_pre[l]) @ w_ffn_in[l], 2, axis=-1)
        f = (jax.nn.silu(gate) * up) @ w_ffn_out[l]
        x = x + rmsnorm(f, g_ffn_post[l])

    return x


CTX_LEN = 256
GRID_W = 64
N_HEADS = 16
HEAD_DIM_2 = D_MODEL // N_HEADS
D_FF_2 = 2816
N_MIXERS = 2
NA_KH_MAX = 8
NA_KW = 16
NA_QC = 16
NA_KBW = 2 * NA_KW
CONV_W = 3
ROPE_BASE = 10000.0
N_MOD = 9
N_NA_LAYERS = (DEPTH + N_MIXERS - 1) // N_MIXERS
N_CONV_LAYERS = DEPTH // N_MIXERS
DN_ALPHA = (2.0 * DEPTH) ** 0.25
DN_BETA = (8.0 * DEPTH) ** -0.25
LN_EPS = 1e-6


def layer_norm(x, g, b):
    xf = x.astype(jnp.float32)
    mu = jnp.mean(xf, axis=-1, keepdims=True)
    var = jnp.mean(jnp.square(xf - mu), axis=-1, keepdims=True)
    return ((xf - mu) * lax.rsqrt(var + LN_EPS)).astype(x.dtype) * g + b

def modulate(x, shift, scale):
    return x * (1 + scale) + shift

def post_norm_update(x, y, gate, res_w, g, b):
    return layer_norm(DN_ALPHA * x + res_w * gate * y, g, b)

def swiglu_ffn(h, w_in, w_out):
    a, u = jnp.split(h @ w_in, 2, axis=-1)
    return (jax.nn.silu(a) * u) @ w_out

def half_step_ffn(x, shift, scale, gate, w_in, w_out, g, b):
    y = swiglu_ffn(modulate(x, shift, scale), w_in, w_out)
    return post_norm_update(x, y, gate, 0.5, g, b)

def axial_rope_tables(n_tok):
    t = np.arange(n_tok)
    n_freq = HEAD_DIM_2 // 4
    inv_freq = ROPE_BASE ** (-np.arange(n_freq) / n_freq)
    ang_row = (t // GRID_W)[:, None] * inv_freq[None]
    ang_col = (t % GRID_W)[:, None] * inv_freq[None]
    return (jnp.asarray(np.cos(ang_row), jnp.float32), jnp.asarray(np.sin(ang_row), jnp.float32),
            jnp.asarray(np.cos(ang_col), jnp.float32), jnp.asarray(np.sin(ang_col), jnp.float32))

def _rotate(x, cos, sin):
    x1, x2 = jnp.split(x, 2, axis=-1)
    cos = cos[None, :, None, :].astype(x.dtype)
    sin = sin[None, :, None, :].astype(x.dtype)
    return jnp.concatenate([x1 * cos - x2 * sin, x2 * cos + x1 * sin], axis=-1)

def apply_axial_rope(x, tables):
    cos_r, sin_r, cos_c, sin_c = tables
    half = HEAD_DIM_2 // 2
    return jnp.concatenate([_rotate(x[..., :half], cos_r, sin_r),
                            _rotate(x[..., half:], cos_c, sin_c)], axis=-1)

def neighbourhood_attention(hx, hc, w_qkv, w_out, rpb, rope, with_ctx_queries):
    B, S, D = hx.shape
    rows = S // GRID_W
    kh = min(NA_KH_MAX, rows)
    ncb = GRID_W // NA_QC
    nk = kh * NA_KBW
    scale = HEAD_DIM_2 ** -0.5

    qkv = (hx @ w_qkv).reshape(B, S, 3, N_HEADS, HEAD_DIM_2)
    q = apply_axial_rope(qkv[:, :, 0], rope)
    k = apply_axial_rope(qkv[:, :, 1], rope)
    v = qkv[:, :, 2]
    qkv_c = (hc @ w_qkv).reshape(B, hc.shape[1], 3, N_HEADS, HEAD_DIM_2)
    q_c, k_c, v_c = qkv_c[:, :, 0], qkv_c[:, :, 1], qkv_c[:, :, 2]

    q_col = np.arange(ncb)[:, None] * NA_QC + np.arange(NA_QC)[None]
    win_c0 = np.clip(q_col - NA_KW // 2, 0, GRID_W - NA_KW)
    blk_c0 = np.clip(np.arange(ncb) * NA_QC - NA_KW // 2, 0, GRID_W - NA_KBW)
    key_col = blk_c0[:, None] + np.arange(NA_KBW)[None]
    col_ok = (key_col[:, None, :] >= win_c0[..., None]) & (key_col[:, None, :] < win_c0[..., None] + NA_KW)
    mask = jnp.asarray(np.broadcast_to(col_ok[:, :, None, :], (ncb, NA_QC, kh, NA_KBW)).reshape(ncb, NA_QC, nk))
    dx_idx = np.clip(key_col[:, None, :] - q_col[..., None] + NA_KW - 1, 0, 2 * NA_KW - 2)
    dx_b = np.broadcast_to(dx_idx[:, :, None, :], (ncb, NA_QC, kh, NA_KBW))

    k_grid = k.reshape(B, rows, GRID_W, N_HEADS, HEAD_DIM_2)
    v_grid = v.reshape(B, rows, GRID_W, N_HEADS, HEAD_DIM_2)
    q_rows = jnp.moveaxis(q.reshape(B, rows, ncb, NA_QC, N_HEADS, HEAD_DIM_2), 1, 0)

    def row_block(args):
        r, q_r = args
        rs = jnp.clip(r - kh // 2, 0, rows - kh)
        k_rows = lax.dynamic_slice_in_dim(k_grid, rs, kh, axis=1)
        v_rows = lax.dynamic_slice_in_dim(v_grid, rs, kh, axis=1)
        k_blk = jnp.moveaxis(k_rows[:, :, key_col], 2, 1).reshape(B, ncb, nk, N_HEADS, HEAD_DIM_2)
        v_blk = jnp.moveaxis(v_rows[:, :, key_col], 2, 1).reshape(B, ncb, nk, N_HEADS, HEAD_DIM_2)
        dy_idx = rs + jnp.arange(kh) - r + NA_KH_MAX - 1
        bias = rpb[:, dy_idx[None, None, :, None], dx_b].reshape(N_HEADS, ncb, NA_QC, nk)
        s_win = jnp.einsum('bjqhd,bjkhd->bhjqk', q_r, k_blk).astype(jnp.float32) * scale
        s_win = jnp.where(mask, s_win + bias.astype(jnp.float32)[None], -jnp.inf)
        s_ctx = jnp.einsum('bjqhd,bchd->bhjqc', q_r, k_c).astype(jnp.float32) * scale
        p = jax.nn.softmax(jnp.concatenate([s_win, s_ctx], axis=-1), axis=-1).astype(v.dtype)
        return (jnp.einsum('bhjqk,bjkhd->bjqhd', p[..., :nk], v_blk)
                + jnp.einsum('bhjqc,bchd->bjqhd', p[..., nk:], v_c))

    o = lax.map(row_block, (jnp.arange(rows), q_rows))
    y_lat = jnp.moveaxis(o, 0, 1).reshape(B, S, D) @ w_out

    y_ctx = None
    if with_ctx_queries:
        s = jnp.einsum('bqhd,bkhd->bhqk', q_c, k_c).astype(jnp.float32) * scale
        p = jax.nn.softmax(s, axis=-1).astype(v_c.dtype)
        y_ctx = jnp.einsum('bhqk,bkhd->bqhd', p, v_c).reshape(B, hc.shape[1], D) @ w_out
    return y_lat, y_ctx

def short_conv_mixer(h, w_in, conv_w, w_out):
    b_gate, c_gate, hv = jnp.split(h @ w_in, 3, axis=-1)
    u = c_gate * hv
    n = u.shape[1]
    pad = CONV_W // 2
    up = jnp.pad(u, ((0, 0), (pad, pad), (0, 0)))
    y = conv_w[0] * up[:, 0:n]
    for j in range(1, CONV_W):
        y = y + conv_w[j] * up[:, j:j + n]
    return (b_gate * y) @ w_out

def second_inputs(seed: int = 0) -> dict:
    key = jax.random.key(seed)
    ks = jax.random.split(key, 16)
    D, F = D_MODEL, D_FF_2

    def nrm(k, shape, s):
        return jax.random.normal(k, shape, jnp.float32) * s

    return {
        "x": nrm(ks[0], (BATCH, SEQ, D), 1.0),
        "c": nrm(ks[1], (BATCH, D), 1.0),
        "ctx": nrm(ks[2], (BATCH, CTX_LEN, D), 1.0),
        "c_ctx": nrm(ks[3], (D,), 1.0),
        "ada_w": nrm(ks[4], (DEPTH, D, N_MOD * D), 0.5 * D ** -0.5),
        "ada_b": nrm(ks[5], (DEPTH, N_MOD * D), 0.02),
        "ln_g": 1.0 + nrm(ks[6], (DEPTH, 3, D), 0.02),
        "ln_b": nrm(ks[7], (DEPTH, 3, D), 0.02),
        "ffn_w_in": nrm(ks[8], (DEPTH, 2, D, 2 * F), D ** -0.5),
        "ffn_w_out": nrm(ks[9], (DEPTH, 2, F, D), DN_BETA * F ** -0.5),
        "na_w_qkv": nrm(ks[10], (N_NA_LAYERS, D, 3 * D), D ** -0.5),
        "na_w_out": nrm(ks[11], (N_NA_LAYERS, D, D), DN_BETA * D ** -0.5),
        "na_rpb": nrm(ks[12], (N_NA_LAYERS, N_HEADS, 2 * NA_KH_MAX - 1, 2 * NA_KW - 1), 0.1),
        "sc_w_in": nrm(ks[13], (N_CONV_LAYERS, D, 3 * D), D ** -0.5),
        "sc_conv": nrm(ks[14], (N_CONV_LAYERS, CONV_W, D), CONV_W ** -0.5),
        "sc_w_out": nrm(ks[15], (N_CONV_LAYERS, D, D), DN_BETA * D ** -0.5),
    }

def second_block(x, c, ctx, c_ctx, ada_w, ada_b, ln_g, ln_b, ffn_w_in, ffn_w_out,
              na_w_qkv, na_w_out, na_rpb, sc_w_in, sc_conv, sc_w_out):
    B, S, D = x.shape
    rope = axial_rope_tables(S)
    last_na = max(range(0, DEPTH, N_MIXERS))
    s_c = jax.nn.silu(c)
    s_cc = jax.nn.silu(c_ctx)
    for i in range(DEPTH):
        ctx_in = i <= last_na
        ctx_out = i < last_na
        j = i // N_MIXERS
        m = (s_c @ ada_w[i] + ada_b[i]).reshape(B, N_MOD, 1, D)
        mc = (s_cc @ ada_w[i] + ada_b[i]).reshape(N_MOD, D)

        x = half_step_ffn(x, m[:, 0], m[:, 1], m[:, 2], ffn_w_in[i, 0], ffn_w_out[i, 0], ln_g[i, 0], ln_b[i, 0])
        if ctx_in:
            ctx = half_step_ffn(ctx, mc[0], mc[1], mc[2], ffn_w_in[i, 0], ffn_w_out[i, 0], ln_g[i, 0], ln_b[i, 0])

        hx = modulate(x, m[:, 3], m[:, 4])
        y_ctx = None
        if i % N_MIXERS == 0:
            hc = modulate(ctx, mc[3], mc[4])
            y_lat, y_ctx = neighbourhood_attention(hx, hc, na_w_qkv[j], na_w_out[j], na_rpb[j], rope, ctx_out)
        else:
            y_lat = short_conv_mixer(hx, sc_w_in[j], sc_conv[j], sc_w_out[j])
            if ctx_out:
                y_ctx = short_conv_mixer(modulate(ctx, mc[3], mc[4]), sc_w_in[j], sc_conv[j], sc_w_out[j])
        x = post_norm_update(x, y_lat, m[:, 5], 1.0, ln_g[i, 1], ln_b[i, 1])
        if ctx_out:
            ctx = post_norm_update(ctx, y_ctx, mc[5], 1.0, ln_g[i, 1], ln_b[i, 1])

        x = half_step_ffn(x, m[:, 6], m[:, 7], m[:, 8], ffn_w_in[i, 1], ffn_w_out[i, 1], ln_g[i, 2], ln_b[i, 2])
        if ctx_out:
            ctx = half_step_ffn(ctx, mc[6], mc[7], mc[8], ffn_w_in[i, 1], ffn_w_out[i, 1], ln_g[i, 2], ln_b[i, 2])
    return x


def setup_inputs(seed=0):
    out = dict(first_inputs(seed))
    for name, value in second_inputs(seed + 1).items():
        if name != "x":
            out[name + "_2"] = value
    return out


def reference(
    x, mem, positions, g_mix_pre, g_mix_post, w_in, diff_lambda, diff_head_g, mla_q_norm_g,
    mla_w_q_up, mla_kv_norm_g, mla_w_kv_up, swa_sinks, w_out, g_x_pre, g_x_mem, g_x_post, w_xq,
    w_xkv, w_xo, g_ffn_pre, g_ffn_post, w_ffn_in, w_ffn_out, c_2, ctx_2, c_ctx_2, ada_w_2,
    ada_b_2, ln_g_2, ln_b_2, ffn_w_in_2, ffn_w_out_2, na_w_qkv_2, na_w_out_2, na_rpb_2,
    sc_w_in_2, sc_conv_2, sc_w_out_2,
):
    x = first_block(
        x, mem, positions, g_mix_pre, g_mix_post, w_in, diff_lambda, diff_head_g, mla_q_norm_g,
        mla_w_q_up, mla_kv_norm_g, mla_w_kv_up, swa_sinks, w_out, g_x_pre, g_x_mem, g_x_post,
        w_xq, w_xkv, w_xo, g_ffn_pre, g_ffn_post, w_ffn_in, w_ffn_out,
    )
    return second_block(
        x, c_2, ctx_2, c_ctx_2, ada_w_2, ada_b_2, ln_g_2, ln_b_2, ffn_w_in_2, ffn_w_out_2,
        na_w_qkv_2, na_w_out_2, na_rpb_2, sc_w_in_2, sc_conv_2, sc_w_out_2,
    )


_drawn_inputs = setup_inputs


def setup_inputs(seed=0):
    import zlib

    import numpy as np

    out = dict(_drawn_inputs(seed))
    spreads = {}
    factors = {'g_mix_post': 2.783,
     'diff_head_g': 3.191,
     'mla_q_norm_g': 8.0,
     'mla_kv_norm_g': 8.0,
     'g_x_pre': 3.321,
     'g_x_post': 3.268,
     'g_ffn_pre': 3.0,
     'g_ffn_post': 4.174,
     'ctx_2': 200.0,
     'ada_b_2': 3.881,
     'na_rpb_2': 64.0,
     'c_ctx_2': 8.0}
    for name, (base, spread) in spreads.items():
        noise = np.random.default_rng([zlib.crc32(name.encode()), seed]).standard_normal(out[name].shape)
        drawn = base * np.exp(spread * noise) if base else spread * noise
        out[name] = jnp.asarray(drawn.astype(out[name].dtype))
    for name, factor in factors.items():
        out[name] = (out[name] * factor).astype(out[name].dtype)
    return out
```

```python
import math
from contextlib import ExitStack, contextmanager

import numpy as np

import concourse.bass as bass
from concourse import mybir

ALU = mybir.AluOpType
ACT = mybir.ActivationFunctionType
F32 = mybir.dt.float32
F32R = mybir.dt.float32r
I32 = mybir.dt.int32
AX = mybir.AxisListType.X

P = 128
D = 1024
SEQ = 256
T = SEQ // P
KC = D // P
DEPTH = 2
GW = 512
UW = 1024
RING = 4
D_FF = 2816
FC = D_FF // P
FG = D_FF // 256
D_IN = 1952
IN_GW = D_IN // 4
EPS = 1e-6

AQ, AK, AV, CQ, CKV, KR, WQ, WK, WV = 0, 256, 512, 768, 1024, 1152, 1184, 1696, 1824
DIFF_H, DIFF_D, DIFF_V = 4, 32, 64
MLA_H, NOPE, ROPE, MLA_V = 4, 64, 32, 64
MLA_D = NOPE + ROPE
SWA_H, SWA_D = 8, 64
X_H, X_D = 4, 256
NA_H, NA_D, GRID = 16, 64, 64
RPB_H, RPB_W = 15, 31
N_ALIBI = DIFF_H + SWA_H
SLOPES = [2.0 ** (-8.0 * (i + 1) / N_ALIBI) for i in range(N_ALIBI)]
ALPHA = (2.0 * DEPTH) ** 0.25
FAR = 1e30

G_MIX, G_X, G_MEM, G_FFN, G_MQ, G_MKV, G_CONV = 0, 16, 32, 48, 64, 68, 70
N_COLS = 94

LAM_INIT = [0.8 - 0.6 * math.exp(-0.3 * l) for l in range(DEPTH)]
ROUND = 1.5 * 2.0 ** 23
TWO_PI = (6.28125, 0.0019350051879882812, 3.0199159795074593e-07)
PI_IN = 3.1415925
START_LOADS = 12

TURN, OUT = 4, 6


class Known:

    def __init__(self, eng, sems):
        self.eng, self.sems = eng, sems
        self.n = {s: 0 for s in sems}
        self.n["units"] = 0
        self.turn = self.steps = self.newest = None

    def at(self, s, value):
        assert value > 0, (s, value)
        if self.turn is None:
            return value
        assert s in self.steps, s
        return self.turn * self.steps[s] + value

    def next(self, s, k=1):
        self.n[s] += k
        return self.at(s, self.n[s])

    def up(self, s, k=1):
        self.n[s] += k
        self.newest = s
        return self.sems[s], k

    def last(self):
        return self.sems[self.newest], self.at(self.newest, self.n[self.newest])

    @contextmanager
    def turns(self, times, **steps):
        before = dict(self.n)
        self.steps, self.newest = steps, None
        with self.eng.Fori(0, times) as i:
            self.turn = i
            yield i
        self.turn = None
        for s, v in self.n.items():
            got = v - before[s]
            assert got == 0 or got == steps.get(s, 0), (s, got, steps.get(s))
            self.n[s] = before[s] + times * got


def spread(ap, n, at=1):
    dims = [tuple(x) for x in ap.ap]
    return bass.AP(ap.tensor, ap.offset, dims[:at] + [(0, n)] + dims[at:])


def build(nc, ins, out):
    ctx = ExitStack()
    with ctx:
        def sb(name, shape, dt=F32, stack=ctx):
            return stack.enter_context(nc.sbuf_tensor(name, shape, dt))

        land = sb("land", [P, RING, UW])
        w_hi = sb("w_hi", [P, RING, UW], F32R)
        w_lo = sb("w_lo", [P, RING, UW], F32R)
        ada_land = sb("ada_land", [P, 4, UW])
        x = sb("x", [P, T, D])
        io = sb("io", [P, T, D])
        z = sb("z", [P, T, D])
        h_hi = sb("h_hi", [P, KC, SEQ], F32R)
        h_lo = sb("h_lo", [P, KC, SEQ], F32R)
        rows = sb("rows", [P, 3, D])
        keysT = sb("keysT", [P, KC, SEQ])
        vals = sb("vals", [P, T, D])
        ident = sb("ident", [P, P])
        cols = sb("cols", [P, N_COLS])
        ccol = sb("ccol", [P, KC, 2])
        mcol = sb("mcol", [P, 3, 72])
        stat = sb("stat", [P, 32])
        mstat = sb("mstat", [P, 5, 32, T])
        dist = sb("dist", [P, T, SEQ])
        dist_w = sb("dist_w", [P, T, SEQ])
        cosb = sb("cosb", [P, T, 16])
        sinb = sb("sinb", [P, T, 16])
        lam = sb("lam", [P, 16])
        newton = sb("newton", [P, 4, 8])
        rope_t = sb("rope_t", [P, 4, MLA_H * 16])
        mrow = sb("mrow", [72, 3, P])
        sinks = sb("sinks", [P, DEPTH, SWA_H])
        ghead = sb("ghead", [P, DEPTH, DIFF_V])
        ada_b = sb("ada_b", [2, 2, GW])
        ada_o = sb("ada_o", [2, 2, GW])
        aff = sb("aff", [P, 2, 2, SEQ])

        def alloc(*specs):
            with ExitStack() as s:
                return [sb(n, shape, dt, s) for n, shape, dt in specs]

        hid_hi, hid_lo, sg, hid = alloc(
            ("hid_hi", [P, FC, SEQ], F32R), ("hid_lo", [P, FC, SEQ], F32R),
            ("sg", [P, T, 256], F32), ("hid", [P, 2, T, 256], F32))
        zin, o, prob, probT, qkT, wk_sw, q96, k96, v_ml = alloc(
            ("zin", [P, T, D_IN], F32), ("o", [P, T, D], F32), ("prob", [P, 2, 512], F32), ("probT", [P, 2, 512], F32),
            ("qkT", [P, 10, SEQ], F32), ("wk_sw", [P, T, P], F32),
            ("q96", [P, T, MLA_H, MLA_D], F32), ("k96", [P, T, MLA_H, MLA_D], F32), ("v_ml", [P, T, MLA_H, MLA_V], F32))
        q96T, k96T = keysT[:, 0:MLA_H, :], keysT[:, MLA_H:2 * MLA_H, :]
        wq_up = vals[:, 0, 0:2 * MLA_H * MLA_D].rearrange("p (k n) -> p k n", k=2)
        wkv_up = vals[:, 1, 0:MLA_H * (NOPE + MLA_V)]
        tok_x, o_x, prob_x, probT_x, qT_x = alloc(
            ("tok_x", [P, T, D], F32), ("o_x", [P, T, D], F32), ("prob_x", [P, 2, 512], F32),
            ("probT_x", [P, 2, 512], F32), ("qT_x", [P, KC, SEQ], F32))
        qkv, prob_n, probT_n, qT_n, kT_n = alloc(
            ("qkv", [P, T, 3 * D], F32), ("prob_n", [P, 2, 512], F32), ("probT_n", [P, 2, 512], F32),
            ("qT_n", [P, KC, SEQ], F32), ("kT_n", [P, KC, SEQ], F32))
        bias_n = ada_land[:, :, 0:T * SEQ].rearrange("p h (t s) -> p h t s", t=T)
        mask_n = ada_land[:, 0, T * SEQ:2 * T * SEQ].rearrange("p (t s) -> p t s", t=T)
        rope_n = ada_land[:, 1, T * SEQ:T * SEQ + 128].rearrange("p (a t g b) -> p a t g b", a=2, t=T, g=2)
        rope_nt = z[:, 0, :].rearrange("p (j n) -> p j n", j=4)
        bch, u_pad, conv_y = alloc(("bch", [P, T, 3 * D], F32), ("u_pad", [P, 2, 2, SEQ + 2], F32),
                                   ("conv_y", [P, 2, SEQ], F32))
        pos_i, pos_c, pos_ci, pos_r, inv16, ang, dl, band, csig, lam_t = alloc(
            ("pos_i", [P, SEQ], I32), ("pos_c", [P, T], F32), ("pos_ci", [P, T], I32), ("pos_r", [P, SEQ], F32),
            ("inv16", [P, 16], F32), ("ang", [P, 4, T, 16], F32), ("dl", [P, DEPTH, 4, DIFF_D], F32),
            ("band", [P, T, SEQ], F32), ("csig", [P, KC, 2], F32), ("lam_t", [P, 4, DIFF_D], F32))

        ps = ctx.enter_context(nc.psum_tensor("ps", [P, 8, 512], F32))

        ada_m = nc.dram_tensor("ada_m", (DEPTH, 2, 9 * D), F32, kind="Internal").ap()
        rpb_w = nc.dram_tensor("rpb_w", (NA_H, GRID, 7, GRID), F32, kind="Internal").ap()

        sem_names = [
            "start_in",
            "landed0", "landed1", "landed2", "landed3",
            "hi_ready",
            "lo_ready",
            "w_used",
            "taken",
            "turned",
            "affine",
            "split_hi",
            "split_lo",
            "copied",
            "squares",
            "rstd",
            "normed",
            "x_new",
            "silu_ready",
            "rows_in",
            "io_in",
            "mla_w_in",
            "shaped",
            "turned_v",
            "normed_v",
            "centred",
            "start_v",
            "mla_sq",
            "mla_mm",
            "scores",
            "max_ready",
            "probs",
            "probs_turned",
            "probs_copied",
            "o_ready",
            "o_taken",
            "o_done",
            "bias_in0", "bias_in1", "bias_in2", "bias_in3",
            "rpb_out",
            "conv_u",
            "ada_in0", "ada_in1", "ada_in2", "ada_in3",
            "ada_bias_in0", "ada_bias_in1",
            "ada_used",
            "ada_sum",
            "ada_stored0", "ada_stored1",
            "mrow_in",
            "mcol",
            "zeroed",
            "dve",
            "sink_exp",
            "start_act",
            "out_stored",
        ]
        sems = {s: ctx.enter_context(nc.semaphore(s)) for s in sem_names}
        def bank(b, n=512):
            return ps[:, b, 0:n]

        def two_banks(b):
            return ps[:, b:b + 2, :].rearrange("p a b -> p (a b)")

        def mixer_maps():
            maps = []
            for h in range(DIFF_H):
                for m in range(2):
                    p0 = (h % 2) * 64 + m * DIFF_D
                    maps.append(dict(
                        kind="A", qk=[(qkT[p0:p0 + DIFF_D, h // 2, :], qkT[p0:p0 + DIFF_D, 2 + h // 2, :])],
                        bias=dist, slope=SLOPES[SWA_H + h], scale=DIFF_D ** -0.5, sink=None,
                        v=[zin[:, s, AV + h * DIFF_V:AV + (h + 1) * DIFF_V] for s in range(T)], d=DIFF_V,
                        o=[o[:, t, h * DIFF_V:(h + 1) * DIFF_V] for t in range(T)], diff=m))
            for h in range(MLA_H):
                maps.append(dict(
                    kind="A", qk=[(q96T[0:MLA_D, h, :], k96T[0:MLA_D, h, :])], bias=None, scale=MLA_D ** -0.5,
                    sink=None, v=[v_ml[:, s, h, :] for s in range(T)], d=MLA_V,
                    o=[o[:, t, 256 + h * MLA_V:256 + (h + 1) * MLA_V] for t in range(T)], diff=None))
            for h in range(SWA_H):
                kv, p0 = h // 4, (h % 2) * 64
                maps.append(dict(
                    kind="A", qk=[(qkT[p0:p0 + SWA_D, 4 + h // 2, :], qkT[p0:p0 + SWA_D, 8 if kv == h % 2 else 9, :])],
                    bias=dist_w, slope=SLOPES[h], scale=SWA_D ** -0.5, sink=h,
                    v=[zin[:, s, WV + kv * SWA_D:WV + (kv + 1) * SWA_D] for s in range(T)], d=SWA_D,
                    o=[o[:, t, 512 + h * SWA_D:512 + (h + 1) * SWA_D] for t in range(T)], diff=None))
            return maps

        def cross_maps():
            return [dict(
                kind="A", qk=[(qT_x[:, 2 * h + c, :], keysT[:, 2 * h + c, :]) for c in range(2)], bias=None,
                scale=X_D ** -0.5, sink=None, v=[vals[:, s, h * X_D:(h + 1) * X_D] for s in range(T)], d=X_D,
                o=[o_x[:, t, h * X_D:(h + 1) * X_D] for t in range(T)], diff=None) for h in range(X_H)]

        def na_maps():
            maps = []
            for h in range(NA_H):
                p0 = (h % 2) * NA_D
                for t in range(T):
                    maps.append(dict(
                        kind="B", t=t, q=qT_n[p0:p0 + NA_D, h // 2, t * P:(t + 1) * P],
                        k=[kT_n[p0:p0 + NA_D, h // 2, :], keysT[p0:p0 + NA_D, h // 2, :]], head=h,
                        scale=NA_D ** -0.5, sink=None,
                        v=[qkv[:, s, 2 * D + h * NA_D:2 * D + (h + 1) * NA_D] for s in range(T)]
                        + [vals[:, s, h * NA_D:(h + 1) * NA_D] for s in range(T)],
                        d=NA_D, o=[qkv[:, t, h * NA_D:(h + 1) * NA_D]], diff=None))
            return maps

        MAPS = {"mixer": (mixer_maps, prob, probT), "cross": (cross_maps, prob_x, probT_x), "na": (na_maps, prob_n, probT_n)}
        TILES = {"x": x, "io": io, "z": z, "o": o, "o_x": o_x, "o_n": qkv}

        def forward(stages):
            def do(name, *args, **kw):
                if name in stages:
                    stages[name](*args, **kw)

            def ffn(w_in, w_out):
                do("ffn_in", w_in)
                do("ffn_out", w_out)

            def modulated_ffn(src, w_in, w_out, mset, first, layer, who, norm):
                do("make_h", src, scale=(mset, first + 1), shift=(mset, first), raw=True)
                do("load_rows", [("ada", layer, who, first + 2), ("ln_g_2", layer, norm), ("ln_b_2", layer, norm)])
                ffn(w_in, w_out)
                do("post_ln", src, 0.5, FC)

            do("start")
            ada_plan = {0: (5, 0, 4, 3, 3, 3), 1: (5, 0, 4, 3, 3, 3)}
            for l in range(DEPTH):
                a = ada_plan[l]
                do("pre_rms", "x")
                do("make_h", "z", gain=G_MIX + 8 * l)
                do("load_rows", [("g_mix_post", l)])
                do("mla_weights", l)
                do("products", f"w_in{l}", 4, IN_GW, "zin")
                do("ada", a[0])
                do("mixer_prep", l)
                do("attend", "mixer", l)
                do("diff_norm", l)
                do("turn_o", "o")
                do("products_y", f"w_out{l}")
                do("ada", a[2])
                do("post_rms", 8)
                do("pre_rms", "io")
                do("make_h", "z", gain=G_MEM + 8 * l)
                do("products", f"w_xkv{l}", 4, GW, "kv_x")
                do("turn_keys", "tok_x", 0, keysT)
                do("pre_rms", "x")
                do("make_h", "z", gain=G_X + 8 * l)
                do("load_rows", [("g_x_post", l)])
                do("products", f"w_xq{l}", 2, GW, "q_x")
                do("ada", a[3])
                do("turn_keys", "tok_x", 0, qT_x)
                do("attend", "cross", l)
                do("turn_o", "o_x")
                do("products_y", f"w_xo{l}")
                do("ada", a[4])
                do("post_rms", 8)
                do("pre_rms", "x")
                do("make_h", "z", gain=G_FFN + 8 * l)
                do("load_rows", [("g_ffn_post", l)])
                ffn(f"w_ffn_in{l}", f"w_ffn_out{l}")
                do("ada", a[5])
                do("post_rms", FC)
            do("ada_columns")
            do("load_io", "ctx_2")
            modulated_ffn("io", "ffn_w_in_200", "ffn_w_out_200", 1, 0, 0, 1, 0)
            do("make_h", "io", scale=(1, 4), shift=(1, 3), raw=True)
            do("products", "na_w_kv", 4, GW, "kv_n")
            do("turn_keys", "qkv", 0, keysT)
            for i in range(DEPTH):
                ms = 0 if i == 0 else 2
                modulated_ffn("x", f"ffn_w_in_2{i}0", f"ffn_w_out_2{i}0", ms, 0, i, 0, 0)
                do("make_h", "x", scale=(ms, 4), shift=(ms, 3), raw=True)
                do("load_rows", [("ada", i, 0, 5), ("ln_g_2", i, 1), ("ln_b_2", i, 1)])
                if i == 0:
                    do("na_tables")
                    do("products", "na_w_qkv", 6, GW, "qkv")
                    do("na_rope")
                    do("turn_keys", "qkv", 0, qT_n)
                    do("turn_keys", "qkv", D, kT_n)
                    do("attend", "na", 0)
                    do("turn_o", "o_n")
                    do("products_y", "na_w_out")
                else:
                    do("products", "sc_w_in", 6, GW, "bch")
                    do("conv")
                    do("products_y", "sc_w_out")
                do("post_ln", "x", 1.0, 8)
                modulated_ffn("x", f"ffn_w_in_2{i}1", f"ffn_w_out_2{i}1", ms, 6, i, 0, 2)
            do("store_x")

        counted = []
        forward({"products": lambda w, groups, width, dst: counted.append(4 * groups), "products_y": lambda w: counted.append(8),
                 "ffn_in": lambda w: counted.append(4 * FG), "ffn_out": lambda w: counted.append(FC)})
        UNITS = sum(counted)

        def product_columns(dst, g, width):
            if dst in ("kv_x", "kv_n"):
                tile = {"kv_x": tok_x, "kv_n": qkv}[dst] if g < 2 else vals
                g %= 2
            else:
                tile = {"zin": zin, "q_x": tok_x, "qkv": qkv, "bch": bch}[dst]
            return tile[:, :, g * width:(g + 1) * width]

        block = ctx.enter_context(nc.Block())

        @block.sync
        def _(sp):
            my = Known(sp, sems)
            ada_done = [0]
            posts = [0]

            def post(*_):
                posts[0] += 1

            def start():
                def load(dst, src):
                    sp.dma_start(dst, src).then_inc(sems["start_in"], 16)
                load(x[:, :, :], ins["x"][0].rearrange("(t p) d -> p t d", p=P))
                load(cols[:, :], ins["cols"])
                load(ident[:, :], ins["ident"])
                load(ccol[:, :, :], ins["ccol"])
                load(io[:, :, :], ins["mem"][0].rearrange("(t p) d -> p t d", p=P))
                load(pos_i[:, :], bass.AP(ins["positions"].tensor, 0, [(0, P), (1, SEQ)]))
                load(pos_ci[:, :], ins["pos_cols"])
                load(inv16[:, :], bass.AP(ins["inv16"].tensor, 0, [(0, P), (1, 16)]))
                load(dl[:, :, :, :].rearrange("p a b c -> p (a b c)"),
                     bass.AP(ins["diff_lambda"].tensor, 0, [(0, P), (1, DEPTH * 4 * DIFF_D)]))
                load(band[:, :, :], ins["band"])
                load(sinks[:, :, :].rearrange("p a b -> p (a b)"),
                     bass.AP(ins["swa_sinks"].tensor, 0, [(0, P), (1, DEPTH * SWA_H)]))
                load(ghead[:, :, :].rearrange("p a b -> p (a b)"),
                     bass.AP(ins["diff_head_g"].tensor, 0, [(0, P), (1, DEPTH * DIFF_V)]))
                for j in range(7):
                    src = bass.AP(ins["na_rpb_2"].tensor, (4 + j) * RPB_W + 15,
                                  [(RPB_H * RPB_W, NA_H), (-1, GRID), (1, GRID)])
                    sp.dma_start(rpb_w[:, :, j, :], src).then_inc(sems["rpb_out"], 16)
                sp.wait_ge(sems["zeroed"], my.next("zeroed"))

            def stream(w, first, count):
                src = ins[w]
                width = src.shape[2]

                def unit(at):
                    u = my.n["units"]
                    my.n["units"] += 1
                    slot = u % RING
                    if u - RING + 1 > 0:
                        sp.wait_ge(sems["lo_ready"], my.at("lo_ready", u - RING + 1))
                    sp.dma_start(land[:, slot, 0:width], at).then_inc(*my.up(f"landed{slot}", 16))

                done = 0
                while done < count and (my.n["units"] < RING or count - done < RING):
                    unit(src[first + done])
                    done += 1
                times = (count - done) // RING
                if times:
                    with my.turns(times, units=RING, lo_ready=RING, **{f"landed{s}": 16 for s in range(RING)}) as i:
                        for j in range(RING):
                            unit(src[bass.ds(i * RING + (first + done + j), 1), :, :].rearrange("o p w -> p (o w)"))
                    done += times * RING
                while done < count:
                    unit(src[first + done])
                    done += 1

            def products(w, groups, width, dst):
                first = 8 if w == "na_w_kv" else 0
                stream("na_w_qkv" if w == "na_w_kv" else w, first, 4 * groups)

            def ada_store():
                g = ada_done[0] - 1
                layer, c = divmod(g, 18)
                sp.wait_ge(sems["ada_sum"], my.next("ada_sum"))
                sp.dma_start(ada_m[layer, :, c * GW:(c + 1) * GW], ada_o[:, g % 2, :]).then_inc(*my.up(f"ada_stored{g % 2}", 16))

            def ada(groups):
                for _ in range(groups):
                    g = ada_done[0]
                    layer, c = divmod(g, 18)
                    for j in range(4):
                        if 4 * (g - 1) + j + 1 > 0:
                            sp.wait_ge(sems["ada_used"], my.at("ada_used", 4 * (g - 1) + j + 1))
                        sp.dma_start(ada_land[:, j, :], ins["ada_w_2"][g * 4 + j]).then_inc(*my.up(f"ada_in{j}", 16))
                    if g >= 1:
                        ada_store()
                    ada_done[0] += 1
                    sp.dma_start(ada_b[:, g % 2, :], bass.AP(
                        ins["ada_b_2"].tensor, layer * 9 * D + c * GW, [(0, 2), (1, GW)])).then_inc(*my.up(f"ada_bias_in{g % 2}", 16))

            def ada_columns():
                ada_store()
                for s in ("ada_stored0", "ada_stored1"):
                    if my.n[s] > 0:
                        sp.wait_ge(sems[s], my.at(s, my.n[s]))
                for s, (layer, who) in enumerate([(0, 0), (0, 1), (1, 0)]):
                    sp.dma_start(mrow[:, s, :],
                                        ada_m[layer, who].rearrange("(v p) -> v p", p=P)).then_inc(*my.up("mrow_in", 16))

            def store_x():
                sp.wait_ge(sems["rpb_out"], my.at("rpb_out", 16 * 7))
                for s in ("ada_stored0", "ada_stored1"):
                    if my.n[s] > 0:
                        sp.wait_ge(sems[s], my.at(s, my.n[s]))
                sp.wait_ge(sems["x_new"], my.next("x_new", T * posts[0]))
                sp.dma_start(out[0].rearrange("(t p) d -> p t d", p=P), x[:, :, :]).then_inc(*my.up("out_stored", 16))
                sp.wait_ge(sems["out_stored"], my.at("out_stored", 16))

            forward({
                "start": start, "products": products, "products_y": lambda w: stream(w, 0, 8),
                "ffn_in": lambda w: stream(w, 0, 4 * FG), "ffn_out": lambda w: stream(w, 0, FC),
                "ada": ada, "ada_columns": ada_columns, "store_x": store_x, "post_rms": post, "post_ln": post,
            })
            assert my.n["units"] == UNITS

        @block.gpsimd
        def _(pool):
            my = Known(pool, sems)
            pool.memset(land[:, :, :], 0.0).then_inc(*my.up("zeroed"))

            def lo():
                u = my.n["units"]
                my.n["units"] += 1
                slot = u % RING
                pool.wait_ge(sems["hi_ready"], my.next("hi_ready"))
                pool.tensor_tensor(w_lo[:, slot, :], land[:, slot, :], w_hi[:, slot, :].bitcast(F32),
                                          ALU.subtract).then_inc(*my.up("lo_ready"))

            with my.turns(UNITS // RING, units=RING, hi_ready=RING, lo_ready=RING):
                for _ in range(RING):
                    lo()
            for _ in range(UNITS % RING):
                lo()

        @block.scalar
        def _(act):
            my = Known(act, sems)
            n = my.n
            n["made"] = 0

            def flat(ap):
                return ap.rearrange("p a b -> p (a b)")

            def split(count):
                def unit():
                    u = n["units"]
                    n["units"] += 1
                    slot = u % RING
                    act.wait_ge(sems[f"landed{slot}"], my.at(f"landed{slot}", 16 * (u // RING + 1)))
                    if u - RING + 1 > 0:
                        act.wait_ge(sems["w_used"], my.at("w_used", u - RING + 1))
                    act.activation(w_hi[:, slot, :], land[:, slot, :], ACT.Copy).then_inc(*my.up("hi_ready"))

                count = min(count, UNITS - n["units"])
                while count and (my.turn is not None or n["units"] < RING or count < 2 * RING):
                    unit()
                    count -= 1
                if count >= 2 * RING:
                    with my.turns(count // RING, units=RING, w_used=RING, hi_ready=RING,
                                  **{f"landed{s}": 16 for s in range(RING)}):
                        for _ in range(RING):
                            unit()
                    count %= RING
                for _ in range(count):
                    unit()

            def start():
                split(RING)
                act.wait_ge(sems["start_in"], my.next("start_in", 16 * START_LOADS))
                act.activation(csig[:, :, :], ccol[:, :, :], ACT.Exp, scale=-1.0).then_inc(*my.up("start_act"))
                act.wait_ge(sems["start_v"], my.next("start_v"))
                act.activation(lam[:, 4:8], lam[:, 0:4], ACT.Exp).then_inc(*my.up("start_act"))
                act.activation(cosb[:, :, :], ang[:, 2, :, :], ACT.Sin).then_inc(*my.up("start_act"))
                act.activation(sinb[:, :, :], ang[:, 1, :, :], ACT.Sin).then_inc(*my.up("start_act"))

            def products(w, groups, width, dst):
                split(4 * groups)
                n["w_used"] += 4 * groups
                n["taken"] += groups

            def ffn_in(w):
                def silu(g):
                    act.wait_ge(sems["w_used"], my.next("w_used", 4))
                    act.wait_ge(sems["taken"], my.at("taken", n["taken"]))
                    n["taken"] += 1
                    b = 2 * (g % 2)
                    act.activation(sg[:, :, :], ps[:, b:b + 2, 0:256], ACT.Silu).then_inc(*my.up("silu_ready"))

                def split_hid(g, at):
                    act.wait_ge(sems["turned"], my.next("turned"))
                    act.activation(flat(hid_hi[:, at, :]), bank(TURN + g % 2), ACT.Copy).then_inc(*my.up("split_hi"))

                split(4)
                with my.turns((FG - 1) // 2, units=8, w_used=8, taken=2, hi_ready=8, silu_ready=2, turned=2, split_hi=2,
                              **{f"landed{s}": 32 for s in range(RING)}) as i:
                    for g in (0, 1):
                        silu(g)
                        split(4)
                        split_hid(g, bass.ds(i * 4 + 2 * g, 2))
                silu(FG - 1)
                split_hid(FG - 1, slice(2 * (FG - 1), 2 * FG))

            def load_rows(what):
                for slot, (name, *at) in enumerate(what):
                    if name == "ada":
                        layer, who, v = at
                        if n["ada_stored0"] == 0:
                            for s in ("ada_stored0", "ada_stored1"):
                                act.wait_ge(sems[s], my.next(s, 16 * 18))
                        src = bass.AP(ada_m.tensor, ((layer * 2 + who) * 9 + v) * D, [(0, P), (1, D)])
                    else:
                        row = at[0] if len(at) == 1 else at[0] * 3 + at[1]
                        src = bass.AP(ins[name].tensor, row * D, [(0, P), (1, D)])
                    act.dma_start(rows[:, slot, :], src).then_inc(*my.up("rows_in", 16))

            def mla_weights(l):
                act.dma_start(wq_up[:, :, :], ins["mla_w_q_up"][l].rearrange("(k p) n -> p k n", p=P)).then_inc(*my.up("mla_w_in", 16))
                act.dma_start(wkv_up[:, :], ins["mla_w_kv_up"][l]).then_inc(*my.up("mla_w_in", 16))

            def load_io(name):
                act.dma_start(io[:, :, :], ins[name][0].rearrange("(t p) d -> p t d", p=P)).then_inc(sems["io_in"], 16)

            def residual(t=T - 1):
                want = n["made"] - (T - 1 - t)
                if n["x_new"] < want:
                    act.wait_ge(sems["x_new"], my.next("x_new", want - n["x_new"]))

            def pre_rms(src):
                tile = TILES[src]
                for t in range(T):
                    residual(t)
                    act.activation(z[:, t, :], tile[:, t, :], ACT.Square, accum_out=stat[:, t:t + 1]).then_inc(*my.up("squares"))
                act.wait_ge(sems["rstd"], my.next("rstd"))
                for t in range(T):
                    act.activation(z[:, t, :], tile[:, t, :], ACT.Copy, scale=stat[:, 8 + t:9 + t]).then_inc(*my.up("normed"))

            def make_h(src, gain=None, scale=None, shift=None, raw=False):
                residual()
                for kp in range(KC // 2):
                    act.wait_ge(sems["affine"], my.next("affine"))
                    act.activation(flat(h_hi[:, 2 * kp:2 * kp + 2, :]), flat(aff[:, kp % 2, :, :]), ACT.Copy).then_inc(*my.up("split_hi"))

            def post(units):
                n["w_used"] += units
                n["taken"] += 2
                n["made"] += T

            def post_rms(units):
                post(units)
                act.wait_ge(sems["w_used"], my.at("w_used", n["w_used"]))
                for t in range(T):
                    act.activation(z[:, t, :], two_banks(2 * t), ACT.Square, accum_out=stat[:, t:t + 1]).then_inc(*my.up("squares"))

            def post_ln(src, res, units):
                post(units)
                for t in range(T):
                    act.wait_ge(sems["centred"], my.next("centred"))
                    if t:
                        act.wait_ge(*my.last())
                    act.activation(aff[:, :, :, :].rearrange("p a b c -> p (a b c)"), z[:, t, :], ACT.Square,
                                          bias=stat[:, 4 + t:5 + t], accum_out=stat[:, t:t + 1]).then_inc(*my.up("squares"))
                act.wait_ge(sems["rstd"], my.next("rstd"))
                for t in range(T):
                    act.activation(z[:, t, :], z[:, t, :], ACT.Identity, scale=stat[:, 8 + t:9 + t],
                                          bias=stat[:, 12 + t:13 + t]).then_inc(*my.up("normed_v"))

            def turn_o(name):
                for kp in range(KC // 2):
                    act.wait_ge(sems["turned"], my.next("turned"))
                    act.activation(flat(h_hi[:, 2 * kp:2 * kp + 2, :]), bank(TURN + kp % 2), ACT.Copy).then_inc(*my.up("split_hi"))

            def copy_pair(dst, kp):
                act.wait_ge(sems["turned"], my.next("turned"))
                act.activation(flat(dst), bank(TURN + kp % 2), ACT.Copy).then_inc(*my.up("copied"))

            def turn_keys(src, col, dst):
                for kp in range(KC // 2):
                    copy_pair(dst[:, 2 * kp:2 * kp + 2, :], kp)

            def mixer_prep(l):
                act.wait_ge(sems["taken"], my.at("taken", n["taken"]))
                for t in range(T):
                    act.activation(z[:, t, 0:256], zin[:, t, CQ:CQ + 256], ACT.Square,
                                          accum_out=stat[:, 16 + t:17 + t]).then_inc(*my.up("mla_sq"))
                    act.activation(z[:, t, 256:384], zin[:, t, CKV:CKV + P], ACT.Square,
                                          accum_out=stat[:, 18 + t:19 + t]).then_inc(*my.up("mla_sq"))
                for kp in range(5):
                    copy_pair(qkT[:, 2 * kp:2 * kp + 2, :], kp)
                for c in range(3):
                    gain = G_MQ + 2 * l + c if c < 2 else G_MKV + l
                    act.wait_ge(sems["turned"], my.next("turned"))
                    act.activation(z[:, 1, c * SEQ:(c + 1) * SEQ], bank(TURN + c % 2, SEQ), ACT.Copy,
                                          scale=cols[:, gain:gain + 1]).then_inc(*my.up("copied"))
                for kp in range(4):
                    dst = (q96T, k96T)[kp // 2]
                    act.wait_ge(sems["turned"], my.next("turned"))
                    act.activation(flat(dst[0:MLA_D, 2 * (kp % 2):2 * (kp % 2) + 2, :]),
                                          ps[0:MLA_D, TURN + kp % 2, :], ACT.Copy).then_inc(*my.up("copied"))

            def attend(which, l):
                make, prob_t, probT_t = MAPS[which]
                maps = make()
                turned0, ready0 = n["probs_turned"], n["o_ready"]

                def exps(m):
                    mp = maps[m]
                    act.wait_ge(sems["max_ready"], my.next("max_ready"))
                    if mp["sink"] is not None:
                        act.activation(mstat[:, 3, m, :], mstat[:, 1, m, :], ACT.Exp,
                                              bias=sinks[:, l, mp["sink"]:mp["sink"] + 1]).then_inc(*my.up("sink_exp"))
                    if turned0 + m - 1 > 0:
                        act.wait_ge(sems["probs_turned"], my.at("probs_turned", turned0 + m - 1))
                    e, s = prob_t[:, m % 2, :], bank(m % 4)
                    if mp["kind"] == "A":
                        for t in range(T):
                            done = act.activation(e[:, t * SEQ:(t + 1) * SEQ], s[:, t * SEQ:(t + 1) * SEQ], ACT.Exp,
                                                  bias=mstat[:, 1, m, t:t + 1], scale=mp["scale"],
                                                  accum_out=mstat[:, 2, m, t:t + 1])
                    else:
                        done = act.activation(e, s, ACT.Exp, bias=mstat[:, 1, m, 0:1], scale=mp["scale"],
                                              accum_out=mstat[:, 2, m, 0:1])
                    done.then_inc(*my.up("probs"))

                def copy(m):
                    act.wait_ge(sems["probs_turned"], my.next("probs_turned"))
                    if ready0 + m - 1 > 0:
                        act.wait_ge(sems["o_ready"], my.at("o_ready", ready0 + m - 1))
                    act.activation(probT_t[:, m % 2, :], bank(TURN + m % 2), ACT.Copy).then_inc(*my.up("probs_copied"))

                for m in range(len(maps) + 1):
                    if m < len(maps):
                        exps(m)
                        if which == "na" and maps[m]["t"] == 1 and maps[m]["head"] + 4 < NA_H:
                            load_bias(maps[m]["head"] + 4)
                    if m >= 1:
                        copy(m - 1)
                n["o_ready"] += len(maps)

            def load_bias(h):
                for r in range(4):
                    act.dma_start(bias_n[(r % 2) * GRID:(r % 2 + 1) * GRID, h % 4, r // 2, :],
                                  rpb_w[h, :, 3 - r:7 - r, :].rearrange("c a b -> c (a b)")
                                  ).then_inc(sems[f"bias_in{h % 4}"], 16)

            def na_tables():
                act.wait_ge(sems["rpb_out"], my.next("rpb_out", 16 * 7))
                for h in range(4):
                    load_bias(h)
                act.dma_start(mask_n[:, :, :], ins["na_mask"]).then_inc(sems["io_in"], 16)
                act.dma_start(ada_land[:, 1, T * SEQ:T * SEQ + 128], ins["na_rope"]).then_inc(sems["io_in"], 16)

            def conv():
                a0 = n["affine"]
                for kp in range(KC // 2 + 1):
                    if kp < KC // 2:
                        act.wait_ge(sems["turned"], my.next("turned"))
                        if a0 + kp - 1 > 0:
                            act.wait_ge(sems["affine"], my.at("affine", a0 + kp - 1))
                        b = (TURN, OUT)[kp % 2]
                        act.activation(u_pad[:, kp % 2, :, 1:SEQ + 1],
                                              bank(b).rearrange("p (a b) -> p a b", a=2), ACT.Copy).then_inc(*my.up("conv_u"))
                    if kp:
                        act.wait_ge(sems["affine"], my.next("affine"))
                        k = kp - 1
                        act.activation(flat(h_hi[:, 2 * k:2 * k + 2, :]), flat(aff[:, k % 2, :, :]), ACT.Copy).then_inc(*my.up("split_hi"))

            forward({
                "start": start, "products": products, "products_y": lambda w: split(8), "ffn_in": ffn_in,
                "ffn_out": lambda w: split(FC), "load_rows": load_rows, "mla_weights": mla_weights,
                "load_io": load_io, "pre_rms": pre_rms, "make_h": make_h, "post_rms": post_rms, "post_ln": post_ln,
                "turn_o": turn_o, "turn_keys": turn_keys, "mixer_prep": mixer_prep, "attend": attend,
                "na_tables": na_tables, "conv": conv,
            })

        @block.vector
        def _(dve):
            my = Known(dve, sems)
            n = my.n
            n["ada"] = 0

            def step(ins_):
                ins_.then_inc(*my.up("dve"))
                dve.wait_ge(*my.last())

            def rsqrt(dst, src, size, width, name="dve"):
                m, guess, sq, half = (newton[:, j, 0:width] for j in range(4))
                step(dve.tensor_scalar(m, src, 1.0 / size, EPS, ALU.mult, ALU.add))
                step(dve.tensor_scalar(guess.bitcast(I32), m.bitcast(I32), 1, None, ALU.arith_shift_right))
                step(dve.tensor_scalar(guess.bitcast(I32), guess.bitcast(I32), -1.0, 1597463007.0, ALU.mult, ALU.add))
                for turn in range(3):
                    step(dve.tensor_tensor(sq, guess, guess, ALU.mult))
                    step(dve.scalar_tensor_tensor(half, sq, -0.5, m, ALU.mult, ALU.mult))
                    last = turn == 2
                    ins_ = dve.scalar_tensor_tensor(dst if last else guess, half, 1.5, guess, ALU.add, ALU.mult)
                    if last:
                        ins_.then_inc(*my.up(name))
                    else:
                        step(ins_)

            def start():
                dve.memset(rope_t[:, :, :], 0.0).then_inc(*my.up("taken", 2))
                dve.wait_ge(sems["start_in"], my.next("start_in", 16 * START_LOADS))
                step(dve.tensor_copy(pos_r[:, :], pos_i[:, :]))
                step(dve.tensor_copy(pos_c[:, :], pos_ci[:, :]))
                for t in range(T):
                    step(dve.tensor_scalar(ang[:, 0, t, :], inv16[:, :], pos_c[:, t:t + 1], None, ALU.mult))
                step(dve.tensor_scalar(ang[:, 3, :, :], ang[:, 0, :, :], 1 / (2 * math.pi), ROUND, ALU.mult, ALU.add))
                step(dve.tensor_scalar(ang[:, 3, :, :], ang[:, 3, :, :], ROUND, None, ALU.subtract))
                for piece in TWO_PI:
                    for t in range(T):
                        step(dve.scalar_tensor_tensor(ang[:, 0, t, :], ang[:, 3, t, :], -piece, ang[:, 0, t, :], ALU.mult, ALU.add))
                step(dve.tensor_scalar(ang[:, 1, :, :], ang[:, 0, :, :], PI_IN, -PI_IN, ALU.min, ALU.max))
                step(dve.scalar_tensor_tensor(ang[:, 2, :, :], ang[:, 1, :, :], -1.0, ang[:, 1, :, :], ALU.mult, ALU.min))
                step(dve.tensor_scalar(ang[:, 2, :, :], ang[:, 2, :, :], math.pi / 2, None, ALU.add))
                for l in range(DEPTH):
                    for j in range(2):
                        step(dve.tensor_tensor(lam_t[:, 2 * l + j, :], dl[:, l, 2 * j, :], dl[:, l, 2 * j + 1, :], ALU.mult))
                dve.tensor_reduce(lam[:, 0:4], lam_t[:, :, :], AX, ALU.add).then_inc(*my.up("start_v"))
                for t in range(T):
                    step(dve.tensor_scalar(dist[:, t, :], pos_r[:, :], pos_c[:, t:t + 1], None, ALU.subtract))
                    step(dve.scalar_tensor_tensor(dist[:, t, :], dist[:, t, :], -1.0, dist[:, t, :], ALU.mult, ALU.max))
                step(dve.tensor_tensor(dist_w[:, :, :], dist[:, :, :], band[:, :, :], ALU.add))
                dve.wait_ge(sems["start_act"], my.next("start_act", 4))
                for l in range(DEPTH):
                    step(dve.tensor_tensor(lam[:, 8 + l:9 + l], lam[:, 5 + 2 * l:6 + 2 * l], lam[:, 4 + 2 * l:5 + 2 * l], ALU.subtract))
                    step(dve.tensor_scalar(lam[:, 8 + l:9 + l], lam[:, 8 + l:9 + l], LAM_INIT[l], None, ALU.subtract))
                step(dve.tensor_scalar(csig[:, :, :], csig[:, :, :], 1.0, None, ALU.add))
                step(dve.reciprocal(csig[:, :, :], csig[:, :, :]))
                dve.tensor_tensor(ccol[:, :, :], ccol[:, :, :], csig[:, :, :], ALU.mult).then_inc(*my.up("start_v"))

            def load_io(name):
                n["io_in"] += 16

            def pre_rms(src):
                dve.wait_ge(sems["squares"], my.next("squares", T))
                rsqrt(stat[:, 8:8 + T], stat[:, 0:T], D, T, "rstd")

            def make_h(src, gain=None, scale=None, shift=None, raw=False):
                def affine(kp):
                    dve.wait_ge(sems["turned_v"], my.next("turned_v"))
                    if kp >= 2:
                        dve.wait_ge(*my.last())
                    for c in range(2):
                        k = 2 * kp + c
                        src_ = ps[:, TURN + kp % 2, c * SEQ:(c + 1) * SEQ]
                        dst = aff[:, kp % 2, c, :]
                        if gain is not None:
                            ins_ = dve.tensor_scalar(dst, src_, cols[:, gain + k:gain + k + 1], None, ALU.mult)
                        else:
                            (s, v), (_, b) = scale, shift
                            ins_ = dve.tensor_scalar(dst, src_, mcol[:, s, v * KC + k:v * KC + k + 1],
                                                     mcol[:, s, b * KC + k:b * KC + k + 1], ALU.mult, ALU.add)
                    ins_.then_inc(*my.up("affine"))

                def lo(kp):
                    dve.wait_ge(sems["split_hi"], my.next("split_hi"))
                    dve.tensor_tensor(h_lo[:, 2 * kp:2 * kp + 2, :], aff[:, kp % 2, :, :],
                                             h_hi[:, 2 * kp:2 * kp + 2, :].bitcast(F32), ALU.subtract).then_inc(*my.up("split_lo"))

                for kp in range(KC // 2 + 1):
                    if kp < KC // 2:
                        affine(kp)
                    if kp:
                        lo(kp - 1)

            def turned_lo(lo_dst, hi_src, kp):
                dve.wait_ge(sems["split_hi"], my.next("split_hi"))
                dve.tensor_tensor(lo_dst, bank(TURN + kp % 2).rearrange("p (a b) -> p a b", a=2),
                                         hi_src.bitcast(F32), ALU.subtract).then_inc(*my.up("split_lo"))

            def turn_o(name):
                for kp in range(KC // 2):
                    turned_lo(h_lo[:, 2 * kp:2 * kp + 2, :], h_hi[:, 2 * kp:2 * kp + 2, :], kp)

            def products(w, groups, width, dst):
                for g in range(groups):
                    dve.wait_ge(sems["w_used"], my.next("w_used", 4))
                    b = 2 * (g % 2)
                    dve.tensor_copy(product_columns(dst, g, width), ps[:, b:b + 2, 0:width]).then_inc(*my.up("taken"))

            def ffn_in(w):
                def gate(g):
                    dve.wait_ge(sems["silu_ready"], my.next("silu_ready"))
                    n["w_used"] += 4
                    b = 2 * (g % 2)
                    dve.tensor_tensor(hid[:, g % 2, :, :], ps[:, b:b + 2, 256:512], sg[:, :, :], ALU.mult).then_inc(*my.up("taken"))

                gate(0)
                with my.turns((FG - 1) // 2, silu_ready=2, w_used=8, taken=2, split_hi=2, split_lo=2) as i:
                    for g in (0, 1):
                        at = bass.ds(i * 4 + 2 * g, 2)
                        turned_lo(hid_lo[:, at, :], hid_hi[:, at, :], g)
                        gate(g + 1)
                turned_lo(hid_lo[:, FC - 2:FC, :], hid_hi[:, FC - 2:FC, :], FG - 1)

            def post_rms(units):
                dve.wait_ge(sems["squares"], my.next("squares", T))
                n["w_used"] += units
                rsqrt(stat[:, 8:8 + T], stat[:, 0:T], D, T)
                dve.wait_ge(*my.last())
                dve.wait_ge(sems["rows_in"], my.next("rows_in", 16))
                for t in range(T):
                    dve.scalar_tensor_tensor(z[:, t, :], two_banks(2 * t), stat[:, 8 + t:9 + t], rows[:, 0, :],
                                                    ALU.mult, ALU.mult).then_inc(*my.up(*(("dve", 1), ("taken", 2))[t]))
                dve.wait_ge(*my.last())
                for t in range(T):
                    dve.tensor_tensor(x[:, t, :], x[:, t, :], z[:, t, :], ALU.add).then_inc(*my.up("x_new"))

            def post_ln(src, res, units):
                tile = TILES[src]
                dve.wait_ge(sems["w_used"], my.next("w_used", units))
                dve.wait_ge(sems["rows_in"], my.next("rows_in", 48))
                for t in range(T):
                    dve.scalar_tensor_tensor(z[:, t, :], two_banks(2 * t), res, rows[:, 0, :],
                                                    ALU.mult, ALU.mult).then_inc(*my.up(*(("dve", 1), ("taken", 2))[t]))
                    dve.wait_ge(*my.last())
                    step(dve.scalar_tensor_tensor(z[:, t, :], tile[:, t, :], ALPHA, z[:, t, :], ALU.mult, ALU.add,
                                                  accum_out=stat[:, 20 + t:21 + t]))
                    dve.tensor_scalar(stat[:, 4 + t:5 + t], stat[:, 20 + t:21 + t], -1.0 / D, None, ALU.mult).then_inc(*my.up("centred"))
                dve.wait_ge(sems["squares"], my.next("squares", T))
                rsqrt(stat[:, 8:8 + T], stat[:, 0:T], D, T)
                dve.wait_ge(*my.last())
                dve.tensor_tensor(stat[:, 12:12 + T], stat[:, 4:4 + T], stat[:, 8:8 + T], ALU.mult).then_inc(*my.up("rstd"))
                for t in range(T):
                    dve.wait_ge(sems["normed_v"], my.next("normed_v"))
                    step(dve.tensor_tensor(tile[:, t, :], z[:, t, :], rows[:, 1, :], ALU.mult))
                    dve.tensor_tensor(tile[:, t, :], tile[:, t, :], rows[:, 2, :], ALU.add).then_inc(*my.up("x_new"))

            def rotate(dst1, dst2, x1, x2, c, s, tmp, name="dve"):
                a, b, d, e = tmp
                step(dve.tensor_tensor(a, x1, c, ALU.mult))
                step(dve.tensor_tensor(b, x2, s, ALU.mult))
                step(dve.tensor_tensor(d, x1, s, ALU.mult))
                step(dve.tensor_tensor(e, x2, c, ALU.mult))
                step(dve.tensor_tensor(dst1, a, b, ALU.subtract))
                dve.tensor_tensor(dst2, d, e, ALU.add).then_inc(*my.up(name))

            def mixer_prep(l):
                dve.wait_ge(*my.last())
                step(dve.tensor_copy(wk_sw[:, :, 0:SWA_D], zin[:, :, WK + SWA_D:WK + 2 * SWA_D]))
                dve.tensor_copy(wk_sw[:, :, SWA_D:P], zin[:, :, WK:WK + SWA_D]).then_inc(*my.up("shaped"))
                dve.wait_ge(sems["mla_sq"], my.next("mla_sq", 2 * T))
                rsqrt(stat[:, 24:26], stat[:, 16:18], 256, T)
                dve.wait_ge(*my.last())
                rsqrt(stat[:, 26:28], stat[:, 18:20], P, T)
                dve.wait_ge(*my.last())
                for t in range(T):
                    step(dve.tensor_scalar(zin[:, t, CQ:CQ + 256], zin[:, t, CQ:CQ + 256], stat[:, 24 + t:25 + t], None, ALU.mult))
                    dve.tensor_scalar(zin[:, t, CKV:CKV + P], zin[:, t, CKV:CKV + P], stat[:, 26 + t:27 + t], None,
                                             ALU.mult).then_inc(*my.up(*(("dve", "shaped")[t],)))
                tmp = [rope_t[:, j, :].rearrange("p (a b) -> p a b", a=MLA_H) for j in range(4)]
                for t in range(T):
                    c, s = spread(cosb[:, t, :], MLA_H), spread(sinb[:, t, :], MLA_H)
                    rotate(k96[:, t, :, NOPE:NOPE + 16], k96[:, t, :, NOPE + 16:MLA_D],
                           spread(zin[:, t, KR:KR + 16], MLA_H), spread(zin[:, t, KR + 16:KR + 32], MLA_H), c, s, tmp)
                dve.wait_ge(sems["mla_mm"], my.next("mla_mm"))
                for t in range(T):
                    q = ps[:, t, 0:MLA_H * MLA_D].rearrange("p (a b) -> p a b", a=MLA_H)
                    kv = ps[:, 2 + t, :].rearrange("p (a b) -> p a b", a=MLA_H)
                    c, s = spread(cosb[:, t, :], MLA_H), spread(sinb[:, t, :], MLA_H)
                    step(dve.tensor_copy(q96[:, t, :, 0:NOPE], q[:, :, 0:NOPE]))
                    step(dve.tensor_copy(k96[:, t, :, 0:NOPE], kv[:, :, 0:NOPE]))
                    step(dve.tensor_copy(v_ml[:, t, :, :], kv[:, :, NOPE:NOPE + MLA_V]))
                    rotate(q96[:, t, :, NOPE:NOPE + 16], q96[:, t, :, NOPE + 16:MLA_D], q[:, :, NOPE:NOPE + 16],
                           q[:, :, NOPE + 16:MLA_D], c, s, tmp, ("dve", "shaped")[t])
                    if t == 0:
                        dve.wait_ge(*my.last())

            def attend(which, l):
                make, _, _ = MAPS[which]
                maps = make()
                if which == "na":
                    dve.wait_ge(sems["io_in"], my.next("io_in", 32))

                def maxima(m):
                    mp = maps[m]
                    s = bank(m % 4)
                    dve.wait_ge(sems["scores"], my.next("scores"))
                    if mp["kind"] == "B":
                        h = mp["head"]
                        dve.wait_ge(sems[f"bias_in{h % 4}"], my.at(f"bias_in{h % 4}", 64 * (h // 4 + 1)))
                        s = s[:, 0:SEQ]
                        step(dve.scalar_tensor_tensor(s, bias_n[:, h % 4, mp["t"], :], 1.0 / mp["scale"], s, ALU.mult, ALU.add))
                        step(dve.tensor_tensor(s, s, mask_n[:, mp["t"], :], ALU.add))
                        step(dve.tensor_reduce(mstat[:, 0, m, 0:1], bank(m % 4), AX, ALU.max))
                        mx, ng = mstat[:, 0, m, 0:1], mstat[:, 1, m, 0:1]
                    else:
                        if mp["bias"] is not None:
                            step(dve.scalar_tensor_tensor(s, mp["bias"][:, :, :].rearrange("p a b -> p (a b)"),
                                                          -mp["slope"] / mp["scale"], s, ALU.mult, ALU.add))
                        step(dve.tensor_reduce(mstat[:, 0, m, :], s.rearrange("p (a b) -> p a b", a=T), AX, ALU.max))
                        mx, ng = mstat[:, 0, m, :], mstat[:, 1, m, :]
                    if mp["sink"] is not None:
                        step(dve.tensor_scalar(mx, mx, mp["scale"], sinks[:, l, mp["sink"]:mp["sink"] + 1], ALU.mult, ALU.max))
                        dve.tensor_scalar(ng, mx, -1.0, None, ALU.mult).then_inc(*my.up("max_ready"))
                    else:
                        dve.tensor_scalar(ng, mx, -mp["scale"], None, ALU.mult).then_inc(*my.up("max_ready"))

                def outputs(m):
                    mp = maps[m]
                    d = mp["d"]
                    dve.wait_ge(sems["o_ready"], my.next("o_ready"))
                    w = len(mp["o"])
                    den, inv = mstat[:, 2, m, 0:w], mstat[:, 4, m, 0:w]
                    if mp["sink"] is not None:
                        step(dve.tensor_tensor(den, den, mstat[:, 3, m, :], ALU.add))
                    step(dve.reciprocal(inv, den))
                    if mp["diff"] == 1:
                        step(dve.tensor_scalar(inv, inv, lam[:, 8 + l:9 + l], None, ALU.mult))
                    for t in range(w):
                        got = ps[:, OUT + m % 2, t * SEQ:t * SEQ + d]
                        if mp["diff"] == 1:
                            ins_ = dve.scalar_tensor_tensor(mp["o"][t], got, inv[:, t:t + 1], mp["o"][t], ALU.mult, ALU.add)
                        else:
                            ins_ = dve.tensor_scalar(mp["o"][t], got, inv[:, t:t + 1], None, ALU.mult)
                    ins_.then_inc(*my.up("o_taken"))

                for m in range(len(maps) + 3):
                    if m < len(maps):
                        maxima(m)
                    if m >= 3:
                        outputs(m - 3)

            def diff_norm(l):
                dve.wait_ge(*my.last())
                for t in range(T):
                    oa, sq = o[:, t, 0:256], z[:, t, 0:256]
                    step(dve.tensor_tensor(sq, oa, oa, ALU.mult))
                    step(dve.tensor_reduce(stat[:, 20 + 4 * t:24 + 4 * t], sq.rearrange("p (a b) -> p a b", a=DIFF_H), AX, ALU.add))
                rsqrt(stat[:, 20:28], stat[:, 20:28], DIFF_V, 8)
                dve.wait_ge(*my.last())
                for t in range(T):
                    oa = o[:, t, 0:256].rearrange("p (a b) -> p a b", a=DIFF_H)
                    step(dve.tensor_tensor(oa, oa, spread(stat[:, 20 + 4 * t:24 + 4 * t], DIFF_V, 2), ALU.mult))
                    dve.scalar_tensor_tensor(oa, oa, 1.0 - LAM_INIT[l], spread(ghead[:, l, :], DIFF_H), ALU.mult, ALU.mult).then_inc(*my.up(("dve", "o_done")[t]))

            def na_rope():
                dve.wait_ge(*my.last())
                dve.wait_ge(sems["io_in"], my.at("io_in", n["io_in"] + 32))
                for t in range(T):
                    for qk in range(2):
                        v = qkv[:, t, qk * D:(qk + 1) * D].rearrange("p (h g a b) -> p h g a b", g=2, a=2, b=16)
                        for g in range(2):
                            c, s = spread(rope_n[:, 0, t, g, :], NA_H), spread(rope_n[:, 1, t, g, :], NA_H)
                            tmp = [rope_nt[:, j, :].rearrange("p (a b) -> p a b", b=16) for j in range(4)]
                            last = t == 1 and qk == 1 and g == 1
                            rotate(v[:, :, g, 0, :], v[:, :, g, 1, :], v[:, :, g, 0, :], v[:, :, g, 1, :], c, s, tmp,
                                   "shaped" if last else "dve")
                            if not last:
                                dve.wait_ge(*my.last())

            def conv():
                dve.wait_ge(*my.last())
                step(dve.memset(u_pad[:, :, :, 0:1], 0.0))
                step(dve.memset(u_pad[:, :, :, SEQ + 1:SEQ + 2], 0.0))
                for t in range(T):
                    dve.tensor_tensor(bch[:, t, D:2 * D], bch[:, t, D:2 * D], bch[:, t, 2 * D:3 * D], ALU.mult).then_inc(*my.up("shaped"))

                def convolve(kp):
                    dve.wait_ge(sems["conv_u"], my.next("conv_u"))
                    dve.wait_ge(*my.last())
                    for c in range(2):
                        k = 2 * kp + c
                        u, y = u_pad[:, kp % 2, c, :], conv_y[:, c, :]
                        w = [cols[:, G_CONV + j * KC + k:G_CONV + j * KC + k + 1] for j in range(3)]
                        step(dve.tensor_scalar(y, u[:, 0:SEQ], w[0], None, ALU.mult))
                        for j in (1, 2):
                            step(dve.scalar_tensor_tensor(y, u[:, j:j + SEQ], w[j], y, ALU.mult, ALU.add))
                        b = (TURN, OUT)[kp % 2] + 1
                        dve.tensor_tensor(aff[:, kp % 2, c, :], y, ps[:, b, c * SEQ:(c + 1) * SEQ], ALU.mult).then_inc(*my.up(("dve", "affine")[c]))
                        if c == 0:
                            dve.wait_ge(*my.last())

                for kp in range(KC // 2 + 1):
                    if kp < KC // 2:
                        convolve(kp)
                    if kp:
                        k = kp - 1
                        dve.wait_ge(sems["split_hi"], my.next("split_hi"))
                        dve.tensor_tensor(h_lo[:, 2 * k:2 * k + 2, :], aff[:, k % 2, :, :],
                                                 h_hi[:, 2 * k:2 * k + 2, :].bitcast(F32), ALU.subtract).then_inc(*my.up("split_lo"))

            def ada(groups):
                for _ in range(groups):
                    g = n["ada"]
                    n["ada"] += 1
                    dve.wait_ge(sems["ada_used"], my.next("ada_used", 4))
                    dve.wait_ge(sems[f"ada_bias_in{g % 2}"], my.next(f"ada_bias_in{g % 2}", 16))
                    if 16 * (g // 2) > 0:
                        dve.wait_ge(sems[f"ada_stored{g % 2}"], my.at(f"ada_stored{g % 2}", 16 * (g // 2)))
                    dve.tensor_tensor(ada_o[:, g % 2, :], ps[0:2, OUT + g % 2, :], ada_b[:, g % 2, :], ALU.add).then_inc(*my.up("ada_sum"))

            def ada_columns():
                dve.wait_ge(sems["turned_v"], my.next("turned_v"))
                step(dve.tensor_copy(mcol[:, :, :], bank(TURN, 3 * P).rearrange("p (a b) -> p a b", a=3)[:, :, 0:72]))
                for v in (1, 4, 7):
                    ins_ = dve.tensor_scalar(mcol[:, :, v * KC:(v + 1) * KC], mcol[:, :, v * KC:(v + 1) * KC], 1.0, None, ALU.add)
                ins_.then_inc(*my.up("mcol"))
                dve.wait_ge(*my.last())

            forward({
                "start": start, "products": products, "ffn_in": ffn_in, "ada": ada, "ada_columns": ada_columns,
                "load_io": load_io, "pre_rms": pre_rms, "make_h": make_h, "post_rms": post_rms, "post_ln": post_ln, "turn_o": turn_o,
                "mixer_prep": mixer_prep, "attend": attend, "diff_norm": diff_norm, "na_rope": na_rope, "conv": conv,
            })

        @block.tensor
        def _(pe):
            my = Known(pe, sems)
            n = my.n
            n["ada"] = n["made"] = 0

            def start():
                pe.wait_ge(sems["start_in"], my.next("start_in", 16 * START_LOADS))
                pe.wait_ge(sems["taken"], my.next("taken", 2))

            def turn_free():
                for s in ("copied", "split_lo", "affine", "probs_copied", "mcol"):
                    if n[s] > 0:
                        pe.wait_ge(sems[s], my.at(s, n[s]))

            def product(u, a, k, left_hi, left_lo, outs, width, first, last):
                slot = u % RING
                for t in range(T):
                    lh, ll = left_hi[:, k, t * P:(t + 1) * P], left_lo[:, k, t * P:(t + 1) * P]
                    for dst, col in outs[t]:
                        wh = w_hi[:, slot, a * width + col:a * width + col + dst.shape[1]]
                        wl = w_lo[:, slot, a * width + col:a * width + col + dst.shape[1]]
                        pe.matmul(dst, lh, wh, start=first, stop=False)
                        pe.matmul(dst, lh, wl, start=False, stop=False)
                        done = pe.matmul(dst, ll, wh, start=False, stop=last)
                return done

            def group(banks, width):
                for j in range(4):
                    u = n["units"]
                    n["units"] += 1
                    pe.wait_ge(sems["lo_ready"], my.at("lo_ready", u + 1))
                    for a in range(2):
                        k = 2 * j + a
                        done = product(u, a, k, h_hi, h_lo, [[(bank(b, width), 0)] for b in banks], width, k == 0, k == KC - 1)
                    done.then_inc(*my.up("w_used"))

            def h_ready():
                if n["split_lo"] > 0:
                    pe.wait_ge(sems["split_lo"], my.at("split_lo", n["split_lo"]))

            def products(w, groups, width, dst):
                h_ready()
                pe.wait_ge(sems["taken"], my.at("taken", n["taken"]))
                if groups >= 4:
                    with my.turns(groups // 2, units=8, lo_ready=8, w_used=8, taken=2):
                        for g in range(2):
                            pe.wait_ge(sems["taken"], my.at("taken", n["taken"] - 1))
                            group((2 * g, 2 * g + 1), width)
                            n["taken"] += 1
                else:
                    for g in range(groups):
                        group((2 * g, 2 * g + 1), width)
                        n["taken"] += 1

            def products_y(w):
                h_ready()
                pe.wait_ge(sems["taken"], my.at("taken", n["taken"]))
                for g in range(2):
                    group((g, 2 + g), GW)

            def turn_hid(g):
                pe.wait_ge(sems["taken"], my.at("taken", n["taken"]))
                if n["split_lo"] - 1 > 0:
                    pe.wait_ge(sems["split_lo"], my.at("split_lo", n["split_lo"] - 1))
                for c in range(2):
                    for t in range(T):
                        done = pe.transpose(ps[:, TURN + g % 2, c * SEQ + t * P:c * SEQ + (t + 1) * P],
                                            hid[:, g % 2, t, c * P:(c + 1) * P], ident[:, :])
                done.then_inc(*my.up("turned"))
                n["split_lo"] += 1

            def ffn_in(w):
                h_ready()
                pe.wait_ge(sems["taken"], my.at("taken", n["taken"]))
                turn_free()
                group((0, 1), GW)
                n["taken"] += 1
                with my.turns((FG - 1) // 2, units=8, lo_ready=8, w_used=8, taken=2, split_lo=2, turned=2):
                    for g in range(2):
                        pe.wait_ge(sems["taken"], my.at("taken", n["taken"] - 1))
                        group(((2, 3), (0, 1))[g], GW)
                        turn_hid(g)
                        n["taken"] += 1
                turn_hid(FG - 1)

            def ffn_out(w):
                h_ready()
                pe.wait_ge(sems["taken"], my.at("taken", n["taken"]))
                for k in range(FC):
                    u = n["units"]
                    n["units"] += 1
                    pe.wait_ge(sems["lo_ready"], my.at("lo_ready", u + 1))
                    outs = [[(bank(2 * t), 0), (bank(2 * t + 1), GW)] for t in range(T)]
                    product(u, 0, k, hid_hi, hid_lo, outs, UW, k == 0, k == FC - 1).then_inc(*my.up("w_used"))

            def post(units):
                n["taken"] += 2
                n["made"] += T

            def turn(tiles, b, name):
                for c, pair in enumerate(tiles):
                    for t, tile in enumerate(pair):
                        m = tile.shape[1]
                        done = pe.transpose(ps[0:m, b, c * SEQ + t * P:c * SEQ + (t + 1) * P], tile, ident[:, :])
                done.then_inc(*my.up(name))

            def pair(tile, col):
                return [[tile[:, t, col + c * P:col + (c + 1) * P] for t in range(T)] for c in range(2)]

            def make_h(src, gain=None, scale=None, shift=None, raw=False):
                turn_free()
                if raw:
                    if src == "io" and n["io_in"] == 0:
                        pe.wait_ge(sems["io_in"], my.next("io_in", 16))
                    elif n["x_new"] < n["made"]:
                        pe.wait_ge(sems["x_new"], my.next("x_new", n["made"] - n["x_new"]))
                else:
                    pe.wait_ge(sems["normed"], my.next("normed", T))
                for kp in range(KC // 2):
                    if kp >= 2:
                        if n["affine"] + kp - 1 > 0:
                            pe.wait_ge(sems["affine"], my.at("affine", n["affine"] + kp - 1))
                    turn(pair(TILES[src], 2 * kp * P), TURN + kp % 2, "turned_v")
                n["affine"] += KC // 2
                n["split_lo"] += KC // 2

            def turn_o(name):
                if name == "o":
                    pe.wait_ge(sems["o_done"], my.next("o_done"))
                if n["o_taken"] > 0:
                    pe.wait_ge(sems["o_taken"], my.at("o_taken", n["o_taken"]))
                turn_free()
                for kp in range(KC // 2):
                    if kp >= 2:
                        pe.wait_ge(sems["split_lo"], my.at("split_lo", n["split_lo"] + kp - 1))
                    turn(pair(TILES[name], 2 * kp * P), TURN + kp % 2, "turned")
                n["split_lo"] += KC // 2

            def turn_keys(src, col, dst):
                tile = {"tok_x": tok_x, "qkv": qkv}[src]
                pe.wait_ge(sems["taken"], my.at("taken", n["taken"]))
                if n["shaped"] > 0:
                    pe.wait_ge(sems["shaped"], my.at("shaped", n["shaped"]))
                turn_free()
                for kp in range(KC // 2):
                    if kp >= 2:
                        if n["copied"] + kp - 1 > 0:
                            pe.wait_ge(sems["copied"], my.at("copied", n["copied"] + kp - 1))
                    turn(pair(tile, col + 2 * kp * P), TURN + kp % 2, "turned")
                n["copied"] += KC // 2

            def na_rope():
                n["shaped"] += 1

            def mixer_prep(l):
                c0 = n["copied"]
                pe.wait_ge(sems["taken"], my.at("taken", n["taken"]))
                turn_free()
                for kp, (i, j) in enumerate(((AQ, AQ + P), (AK, AK + P), (WQ, WQ + P), (WQ + 2 * P, WQ + 3 * P), (WK, None))):
                    if j is None:
                        pe.wait_ge(sems["shaped"], my.next("shaped"))
                    if c0 + kp - 1 > 0:
                        pe.wait_ge(sems["copied"], my.at("copied", c0 + kp - 1))
                    turn([[zin[:, t, i:i + P] for t in range(T)],
                          [wk_sw[:, t, :] if j is None else zin[:, t, j:j + P] for t in range(T)]], TURN + kp % 2, "turned")
                pe.wait_ge(sems["shaped"], my.next("shaped"))
                if c0 + 5 > 0:
                    pe.wait_ge(sems["copied"], my.at("copied", c0 + 5))
                for c, col in enumerate((CQ, CQ + P, CKV)):
                    if c0 + 5 + c - 1 > 0:
                        pe.wait_ge(sems["copied"], my.at("copied", c0 + 5 + c - 1))
                    turn([[zin[:, t, col:col + P] for t in range(T)]], TURN + c % 2, "turned")
                if c0 + 8 > 0:
                    pe.wait_ge(sems["copied"], my.at("copied", c0 + 8))
                pe.wait_ge(sems["mla_w_in"], my.next("mla_w_in", 32))
                for t in range(T):
                    for c in range(2):
                        pe.matmul(ps[:, t, 0:MLA_H * MLA_D], z[:, 1, c * SEQ + t * P:c * SEQ + (t + 1) * P], wq_up[:, c, :],
                                  start=(c == 0), stop=(c == 1))
                    done = pe.matmul(bank(2 + t), z[:, 1, 2 * SEQ + t * P:2 * SEQ + (t + 1) * P], wkv_up[:, :], start=True, stop=True)
                done.then_inc(*my.up("mla_mm"))
                pe.wait_ge(sems["shaped"], my.next("shaped"))
                for kp in range(4):
                    if kp >= 2:
                        if c0 + 8 + kp - 1 > 0:
                            pe.wait_ge(sems["copied"], my.at("copied", c0 + 8 + kp - 1))
                    src, h = (q96, k96)[kp // 2], 2 * (kp % 2)
                    turn([[src[:, t, h + c, :] for t in range(T)] for c in range(2)], TURN + kp % 2, "turned")
                n["copied"] = c0 + 12

            def attend(which, l):
                make, prob_t, probT_t = MAPS[which]
                maps = make()
                p0, c0, o0 = n["probs"], n["probs_copied"], n["o_taken"]
                pe.wait_ge(sems["taken"], my.at("taken", n["taken"]))
                turn_free()

                def score(m):
                    mp = maps[m]
                    if m >= 4:
                        pe.wait_ge(sems["probs"], my.at("probs", p0 + m - 3))
                    if mp["kind"] == "A":
                        for t in range(T):
                            for c, (q, k) in enumerate(mp["qk"]):
                                done = pe.matmul(ps[:, m % 4, t * SEQ:(t + 1) * SEQ], q[:, t * P:(t + 1) * P], k,
                                                 start=(c == 0), stop=(c == len(mp["qk"]) - 1))
                    else:
                        for c, k in enumerate(mp["k"]):
                            done = pe.matmul(ps[:, m % 4, c * SEQ:(c + 1) * SEQ], mp["q"], k, start=True, stop=True)
                    done.then_inc(*my.up("scores"))

                def turn_probs(m):
                    pe.wait_ge(sems["probs"], my.at("probs", p0 + m + 1))
                    if m >= 2:
                        pe.wait_ge(sems["probs_copied"], my.at("probs_copied", c0 + m - 1))
                    e = prob_t[:, m % 2, :]
                    for j in range(4):
                        at = (j % 2) * 2 + j // 2 if maps[m]["kind"] == "A" else j
                        done = pe.transpose(ps[:, TURN + m % 2, at * P:(at + 1) * P], e[:, j * P:(j + 1) * P], ident[:, :])
                    done.then_inc(*my.up("probs_turned"))

                def weigh(m):
                    mp = maps[m]
                    pe.wait_ge(sems["probs_copied"], my.at("probs_copied", c0 + m + 1))
                    if m >= 2:
                        pe.wait_ge(sems["o_taken"], my.at("o_taken", o0 + m - 1))
                    e, nv = probT_t[:, m % 2, :], len(mp["v"])
                    for t in range(len(mp["o"])):
                        for s in range(nv):
                            at = s * 2 + t if mp["kind"] == "A" else s
                            done = pe.matmul(ps[:, OUT + m % 2, t * SEQ:t * SEQ + mp["d"]], e[:, at * P:(at + 1) * P],
                                             mp["v"][s], start=(s == 0), stop=(s == nv - 1))
                    done.then_inc(*my.up("o_ready"))

                for m in range(len(maps) + 2):
                    if m < len(maps):
                        score(m)
                    if 1 <= m <= len(maps):
                        turn_probs(m - 1)
                    if m >= 2:
                        weigh(m - 2)
                n["probs"] += len(maps)
                n["probs_copied"] += len(maps)
                n["o_taken"] += len(maps)

            def conv():
                a0 = n["affine"]
                pe.wait_ge(sems["taken"], my.at("taken", n["taken"]))
                pe.wait_ge(sems["shaped"], my.next("shaped", T))
                turn_free()
                for kp in range(KC // 2):
                    b = (TURN, OUT)[kp % 2]
                    if kp >= 2:
                        if a0 + kp - 1 > 0:
                            pe.wait_ge(sems["affine"], my.at("affine", a0 + kp - 1))
                    for c in range(2):
                        for t in range(T):
                            pe.transpose(ps[:, b + 1, c * SEQ + t * P:c * SEQ + (t + 1) * P],
                                         bch[:, t, (2 * kp + c) * P:(2 * kp + c + 1) * P], ident[:, :])
                    turn(pair(bch, D + 2 * kp * P), b, "turned")
                n["affine"] += KC // 2
                n["split_lo"] += KC // 2

            def ada(groups):
                for _ in range(groups):
                    g = n["ada"]
                    n["ada"] += 1
                    if g == 0:
                        pe.wait_ge(sems["start_v"], my.next("start_v", 2))
                    if n["o_taken"] > 0:
                        pe.wait_ge(sems["o_taken"], my.at("o_taken", n["o_taken"]))
                    if g - 1 > 0:
                        pe.wait_ge(sems["ada_sum"], my.at("ada_sum", g - 1))
                    for j in range(4):
                        pe.wait_ge(sems[f"ada_in{j}"], my.next(f"ada_in{j}", 16))
                        for a in range(2):
                            k = 2 * j + a
                            done = pe.matmul(ps[0:2, OUT + g % 2, :], ccol[:, k, :], ada_land[:, j, a * GW:(a + 1) * GW],
                                             start=(k == 0), stop=(k == KC - 1))
                        done.then_inc(*my.up("ada_used"))

            def ada_columns():
                turn_free()
                pe.wait_ge(sems["mrow_in"], my.next("mrow_in", 48))
                for s in range(3):
                    done = pe.transpose(ps[:, TURN, s * P:s * P + 72], mrow[:, s, :], ident[0:72, 0:72])
                done.then_inc(*my.up("turned_v"))
                n["mcol"] += 1

            forward({
                "start": start, "products": products, "products_y": products_y, "ffn_in": ffn_in, "ffn_out": ffn_out,
                "post_rms": post, "post_ln": lambda src, res, units: post(units), "make_h": make_h, "turn_o": turn_o,
                "turn_keys": turn_keys, "na_rope": na_rope, "mixer_prep": mixer_prep, "attend": attend, "conv": conv,
                "ada": ada, "ada_columns": ada_columns,
            })


def by_columns(w, width):
    n = w.shape[-1] // width
    return np.ascontiguousarray(w.reshape(4, 2, P, n, width).transpose(3, 0, 2, 1, 4)).reshape(n * 4, P, 2 * width)


def gate_up(w):
    return by_columns(w.reshape(D, 2, FG, 256).transpose(0, 2, 1, 3).reshape(D, 2 * D_FF), GW)


def columns(*vectors):
    return np.concatenate([v.reshape(-1, P).T for v in vectors], axis=1)


def constants():
    f = np.float32
    i, j = np.arange(SEQ)[:, None], np.arange(SEQ)[None, :]
    band = np.where(np.abs(i - j) <= 128, 0.0, FAR).astype(f)
    col, key = np.arange(SEQ) % GRID, np.arange(SEQ) % GRID
    w0 = np.clip(col - 8, 0, GRID - 16)[:, None]
    na_mask = np.where((key[None] >= w0) & (key[None] < w0 + 16), 0.0, -FAR).astype(f)
    inv = 10000.0 ** (-np.arange(16) / 16)
    tok = np.arange(SEQ)
    angles = np.stack([(tok // GRID)[:, None] * inv, (tok % GRID)[:, None] * inv], axis=1)
    rope = np.stack([np.cos(angles), np.sin(angles)]).astype(f)
    rope = rope.reshape(2, T, P, 2, 16).transpose(2, 0, 1, 3, 4).reshape(P, -1)
    blocks = lambda a: np.ascontiguousarray(a.reshape(T, P, SEQ).transpose(1, 0, 2))
    return {"ident": np.eye(P, dtype=f), "band": blocks(band), "na_mask": blocks(na_mask), "na_rope": np.ascontiguousarray(rope),
            "inv16": (f(10000.0) ** (-np.arange(16, dtype=f) / f(16))).astype(f)}


def kernel(**inputs):
    import concourse.bacc as _bacc
    from concourse.bass_utils import run_bass_kernel_spmd as _run

    v = {k: np.asarray(a) for k, a in inputs.items()}
    arrays = {k: v[k] for k in ("x", "mem", "positions", "diff_lambda", "diff_head_g", "swa_sinks", "mla_w_q_up",
                                "mla_w_kv_up", "g_mix_post", "g_x_post", "g_ffn_post", "ctx_2", "ada_b_2", "ln_g_2",
                                "ln_b_2", "na_rpb_2")}
    arrays["cols"] = columns(*v["g_mix_pre"], *v["g_x_pre"], *v["g_x_mem"], *v["g_ffn_pre"], *v["mla_q_norm_g"],
                             *v["mla_kv_norm_g"], *v["sc_conv_2"][0])
    arrays["ccol"] = np.stack([v["c_2"][0].reshape(KC, P), v["c_ctx_2"].reshape(KC, P)]).transpose(2, 1, 0)
    arrays["pos_cols"] = v["positions"].reshape(T, P).T
    for l in range(DEPTH):
        arrays[f"w_in{l}"] = by_columns(v["w_in"][l], IN_GW)
        for name in ("w_out", "w_xq", "w_xkv", "w_xo"):
            arrays[f"{name}{l}"] = by_columns(v[name][l], GW)
        arrays[f"w_ffn_in{l}"] = gate_up(v["w_ffn_in"][l])
        arrays[f"w_ffn_out{l}"] = v["w_ffn_out"][l].reshape(FC, P, D)
        for j in range(2):
            arrays[f"ffn_w_in_2{l}{j}"] = gate_up(v["ffn_w_in_2"][l, j])
            arrays[f"ffn_w_out_2{l}{j}"] = v["ffn_w_out_2"][l, j].reshape(FC, P, D)
    arrays["ada_w_2"] = np.concatenate([by_columns(w, GW) for w in v["ada_w_2"]])
    arrays["na_w_qkv"], arrays["na_w_out"] = by_columns(v["na_w_qkv_2"][0], GW), by_columns(v["na_w_out_2"][0], GW)
    arrays["sc_w_in"], arrays["sc_w_out"] = by_columns(v["sc_w_in_2"][0], GW), by_columns(v["sc_w_out_2"][0], GW)
    arrays.update(constants())
    arrays = {k: np.ascontiguousarray(a) for k, a in arrays.items()}

    nc = _bacc.Bacc("TRN2", target_bir_lowering=False, num_devices=1)
    ins = {k: nc.dram_tensor(k + "_dram", a.shape, mybir.dt.from_np(a.dtype), kind="ExternalInput").ap()
           for k, a in arrays.items()}
    out = nc.dram_tensor("out_dram", (1, SEQ, D), F32, kind="ExternalOutput").ap()
    build(nc, ins, out)
    got = _run(nc, [{k + "_dram": a for k, a in arrays.items()}], core_ids=[0])
    return got.results[0]["out_dram"]
```
